# Optimizing a Trainium2 kernel written in Bass

```python
import jax
import jax.numpy as jnp
from jax import lax
import numpy as np
import jax, jax.numpy as jnp

D_MODEL = 2048
BATCH = 1
SEQ = 256
DEPTH = 1

HEAD_DIM = 128
A_GROUPS = 4
A_WIDTH = A_GROUPS * HEAD_DIM
CHUNK = 128
B_HEADS = 4
DILATED_PAIRS = ((128, 1), (512, 4), (2048, 16))
C_HEADS = 8
C_KV_HEADS = 2
C_GROUP = C_HEADS // C_KV_HEADS
CMP_LEN = 32
CMP_STRIDE = 16
SEL_LEN = 64
SEL_TOP = 16
WIN_LEN = 512
NSA_QBLOCK = 64
BAND_BLOCK = 128
MIX_WIDTH = A_WIDTH + (B_HEADS + C_HEADS) * HEAD_DIM
IN_SPLITS = (2 * A_WIDTH,
             3 * B_HEADS * HEAD_DIM,
             C_HEADS * HEAD_DIM,
             2 * C_KV_HEADS * HEAD_DIM,
             2 * C_KV_HEADS * HEAD_DIM,
             2 * C_KV_HEADS * HEAD_DIM,
             3 * C_HEADS)
IN_WIDTH = sum(IN_SPLITS)
N_MEM = 256
X_HEADS = 4
X_WIDTH = X_HEADS * HEAD_DIM
D_FF = 4 * D_MODEL
EPS = 1e-6
NEG_INF = -1e30


def rms_norm(x, g):
    xf = x.astype(jnp.float32)
    y = xf * lax.rsqrt(jnp.mean(xf * xf, axis=-1, keepdims=True) + EPS)
    return (y * g.astype(jnp.float32)).astype(x.dtype)

def layer_norm(x, g, b):
    xf = x.astype(jnp.float32)
    xc = xf - jnp.mean(xf, axis=-1, keepdims=True)
    y = xc * lax.rsqrt(jnp.mean(xc * xc, axis=-1, keepdims=True) + EPS)
    return (y * g.astype(jnp.float32) + b.astype(jnp.float32)).astype(x.dtype)

def banded_attention(q, k, v, max_dist):
    bsz, ng, nr, L, hd = q.shape
    blk = BAND_BLOCK
    nprev = -(-max_dist // blk)
    nb = -(-L // blk)
    pad = nb * blk - L
    qb = jnp.pad(q, ((0, 0), (0, 0), (0, 0), (0, pad), (0, 0))).reshape(bsz, ng, nr, nb, blk, hd)

    def windows(t):
        tb = jnp.pad(t, ((0, 0), (0, 0), (nprev * blk, pad), (0, 0))).reshape(bsz, ng, nb + nprev, blk, hd)
        return jnp.concatenate([tb[:, :, i:i + nb] for i in range(nprev + 1)], axis=3)

    kw, vw = windows(k), windows(v)
    s = jnp.einsum('bgrnqd,bgnkd->bgrnqk', qb, kw).astype(jnp.float32) * (hd ** -0.5)
    qpos = jnp.arange(nb)[:, None] * blk + jnp.arange(blk)[None, :]
    kpos = (jnp.arange(nb)[:, None] - nprev) * blk + jnp.arange((nprev + 1) * blk)[None, :]
    dist = qpos[:, :, None] - kpos[:, None, :]
    mask = (dist >= 0) & (dist <= max_dist) & (kpos[:, None, :] >= 0)
    s = jnp.where(mask, s, NEG_INF)
    m = jnp.max(s, axis=-1, keepdims=True)
    e = jnp.exp(s - m)
    den = jnp.sum(e, axis=-1, keepdims=True)
    o = jnp.einsum('bgrnqk,bgnkd->bgrnqd', (e / den).astype(v.dtype), vw)
    lse = (m + jnp.log(den))[..., 0]
    o = o.reshape(bsz, ng, nr, nb * blk, hd)[:, :, :, :L]
    lse = lse.reshape(bsz, ng, nr, nb * blk)[:, :, :, :L]
    return o, lse

def spatial_gating(uv, ln_g, ln_b, w_s, b_s):
    bsz, S, _ = uv.shape
    u, v = jnp.split(jax.nn.gelu(uv), 2, axis=-1)
    v = layer_norm(v, ln_g, ln_b).reshape(bsz, S // CHUNK, CHUNK, A_GROUPS, HEAD_DIM)
    w = w_s * jnp.tril(jnp.ones((CHUNK, CHUNK), w_s.dtype))
    sv = jnp.einsum('gts,bcsgh->bctgh', w, v) + b_s.T[:, :, None]
    return u * sv.reshape(bsz, S, A_WIDTH)

def dilated_attention(q, k, v):
    bsz, nh, S, hd = q.shape
    outs, lses = [], []
    for window, d in DILATED_PAIRS:
        def fold(t):
            return t.reshape(bsz, nh, S // d, d, hd).transpose(0, 1, 3, 2, 4).reshape(bsz, nh * d, S // d, hd)
        o, l = banded_attention(fold(q)[:, :, None], fold(k), fold(v), window // d)
        outs.append(o[:, :, 0].reshape(bsz, nh, d, S // d, hd).transpose(0, 1, 3, 2, 4).reshape(bsz, nh, S, hd))
        lses.append(l[:, :, 0].reshape(bsz, nh, d, S // d).transpose(0, 1, 3, 2).reshape(bsz, nh, S))
    w = jax.nn.softmax(jnp.stack(lses), axis=0)
    o = jnp.einsum('pbhs,pbhsd->bhsd', w.astype(q.dtype), jnp.stack(outs))
    return o.transpose(0, 2, 1, 3).reshape(bsz, S, nh * hd)

def compress_blocks(kraw, pos, w1, w2):
    bsz, ng, S, hd = kraw.shape
    sub = kraw.reshape(bsz, ng, S // CMP_STRIDE, CMP_STRIDE, hd)
    blocks = jnp.concatenate([sub[:, :, :-1], sub[:, :, 1:]], axis=3) + pos
    n_c = blocks.shape[2]
    h = jax.nn.gelu(blocks.reshape(bsz, ng, n_c, CMP_LEN * hd) @ w1)
    return h @ w2

def nsa_attention(q, kv_cmp, kv_slc, kv_win, gates, cmp_pos, ck_w1, ck_w2, cv_w1, cv_w2):
    bsz, ng, nr, S, hd = q.shape
    scale = hd ** -0.5
    k_c = compress_blocks(kv_cmp[0], cmp_pos, ck_w1, ck_w2)
    v_c = compress_blocks(kv_cmp[1], cmp_pos, cv_w1, cv_w2)
    n_c = k_c.shape[2]
    n_sel = S // SEL_LEN
    n_top = min(SEL_TOP, n_sel)
    k_s = kv_slc[0].reshape(bsz, ng, n_sel, SEL_LEN, hd)
    v_s = kv_slc[1].reshape(bsz, ng, n_sel, SEL_LEN, hd)
    c_start = np.arange(n_c) * CMP_STRIDE
    s_start = np.arange(n_sel) * SEL_LEN
    overlap = jnp.asarray(((c_start[:, None] <= s_start[None, :] + SEL_LEN - 1)
                           & (c_start[:, None] + CMP_LEN - 1 >= s_start[None, :])).astype(np.float32))
    c_end = jnp.arange(n_c) * CMP_STRIDE + CMP_LEN - 1
    sel_idx = jnp.arange(n_sel)
    b_idx = jnp.arange(bsz)[:, None, None, None]
    g_idx = jnp.arange(ng)[None, :, None, None]
    nqb = S // NSA_QBLOCK
    q_blocks = q.reshape(bsz, ng, nr, nqb, NSA_QBLOCK, hd).transpose(3, 0, 1, 2, 4, 5)

    def block_step(args):
        qb, bi = args
        t = bi * NSA_QBLOCK + jnp.arange(NSA_QBLOCK)
        valid_c = c_end[None, :] <= t[:, None]
        s_c = jnp.einsum('bgrqd,bgnd->bgrqn', qb, k_c).astype(jnp.float32) * scale
        p_c = jax.nn.softmax(jnp.where(valid_c, s_c, NEG_INF), axis=-1) * valid_c
        o_c = jnp.einsum('bgrqn,bgnd->bgrqd', p_c.astype(v_c.dtype), v_c)
        imp = jnp.einsum('bgrqn,nj->bgqj', p_c, overlap)
        jt = t // SEL_LEN
        forced = (sel_idx[None] == 0) | (sel_idx[None] == jt[:, None]) | (sel_idx[None] == jt[:, None] - 1)
        valid_s = sel_idx[None] * SEL_LEN <= t[:, None]
        score = jnp.where(forced, 1e4, jnp.where(valid_s, imp, -1.0))
        _, idx = lax.top_k(score, n_top)
        ks = k_s[b_idx, g_idx, idx]
        vs = v_s[b_idx, g_idx, idx]
        kpos = idx[..., None] * SEL_LEN + jnp.arange(SEL_LEN)
        mask_s = (kpos <= t[None, None, :, None, None])[:, :, None]
        s_s = jnp.einsum('bgrqd,bgqnkd->bgrqnk', qb, ks).astype(jnp.float32) * scale
        s_s = jnp.where(mask_s, s_s, NEG_INF).reshape(bsz, ng, nr, NSA_QBLOCK, n_top * SEL_LEN)
        p_s = jax.nn.softmax(s_s, axis=-1).reshape(bsz, ng, nr, NSA_QBLOCK, n_top, SEL_LEN)
        o_s = jnp.einsum('bgrqnk,bgqnkd->bgrqd', p_s.astype(vs.dtype), vs)
        return o_c, o_s

    o_c, o_s = lax.map(block_step, (q_blocks, jnp.arange(nqb)))
    o_c = o_c.transpose(1, 2, 3, 0, 4, 5).reshape(bsz, ng, nr, S, hd)
    o_s = o_s.transpose(1, 2, 3, 0, 4, 5).reshape(bsz, ng, nr, S, hd)
    o_w, _ = banded_attention(q, kv_win[0], kv_win[1], WIN_LEN - 1)
    g = jax.nn.sigmoid(gates.astype(jnp.float32)).reshape(bsz, S, ng, nr, 3)
    g = g.transpose(4, 0, 2, 3, 1)[..., None].astype(q.dtype)
    o = g[0] * o_c + g[1] * o_s + g[2] * o_w
    return o.transpose(0, 3, 1, 2, 4).reshape(bsz, S, ng * nr * hd)

def first_inputs(seed: int = 0) -> dict:
    key = jax.random.key(seed)
    ks = jax.random.split(key, 24)
    f32 = jnp.float32

    def normal(k, shape, scale):
        return jax.random.normal(k, shape, f32) * scale

    def gain(k, shape):
        return 1.0 + normal(k, shape, 0.02)

    L = DEPTH
    return {
        'x': normal(ks[0], (BATCH, SEQ, D_MODEL), 1.0),
        'mem': normal(ks[1], (BATCH, N_MEM, D_MODEL), 1.0),
        'norm_mix': gain(ks[2], (L, D_MODEL)),
        'w_in': normal(ks[3], (L, D_MODEL, IN_WIDTH), D_MODEL ** -0.5),
        'gmlp_ln_g': gain(ks[4], (L, A_WIDTH)),
        'gmlp_ln_b': normal(ks[5], (L, A_WIDTH), 0.02),
        'gmlp_w_s': normal(ks[6], (L, A_GROUPS, CHUNK, CHUNK), CHUNK ** -0.5),
        'gmlp_b_s': gain(ks[7], (L, A_GROUPS, CHUNK)),
        'cmp_pos': normal(ks[8], (L, CMP_LEN, HEAD_DIM), 0.02),
        'cmp_k_w1': normal(ks[9], (L, CMP_LEN * HEAD_DIM, HEAD_DIM), (CMP_LEN * HEAD_DIM) ** -0.5),
        'cmp_k_w2': normal(ks[10], (L, HEAD_DIM, HEAD_DIM), HEAD_DIM ** -0.5),
        'cmp_v_w1': normal(ks[11], (L, CMP_LEN * HEAD_DIM, HEAD_DIM), (CMP_LEN * HEAD_DIM) ** -0.5),
        'cmp_v_w2': normal(ks[12], (L, HEAD_DIM, HEAD_DIM), HEAD_DIM ** -0.5),
        'w_out': normal(ks[13], (L, MIX_WIDTH, D_MODEL), 0.5 * MIX_WIDTH ** -0.5),
        'norm_xattn': gain(ks[14], (L, D_MODEL)),
        'norm_mem': gain(ks[15], (L, D_MODEL)),
        'xattn_wq': normal(ks[16], (L, D_MODEL, X_WIDTH), D_MODEL ** -0.5),
        'xattn_wkv': normal(ks[17], (L, D_MODEL, 2 * X_WIDTH), D_MODEL ** -0.5),
        'xattn_wo': normal(ks[18], (L, X_WIDTH, D_MODEL), 0.5 * X_WIDTH ** -0.5),
        'norm_mlp': gain(ks[19], (L, D_MODEL)),
        'w_up': normal(ks[20], (L, D_MODEL, D_FF), D_MODEL ** -0.5),
        'w_down': normal(ks[21], (L, D_FF, D_MODEL), 0.5 * D_FF ** -0.5),
        'final_norm': gain(ks[22], (D_MODEL,)),
    }

def first_block(x, mem, norm_mix, w_in, gmlp_ln_g, gmlp_ln_b, gmlp_w_s, gmlp_b_s, cmp_pos,
              cmp_k_w1, cmp_k_w2, cmp_v_w1, cmp_v_w2, w_out, norm_xattn, norm_mem,
              xattn_wq, xattn_wkv, xattn_wo, norm_mlp, w_up, w_down, final_norm):
    bsz, S, _ = x.shape
    n_mem = mem.shape[1]
    split_at = [int(i) for i in np.cumsum(IN_SPLITS)[:-1]]
    x_scale = HEAD_DIM ** -0.5
    for l in range(DEPTH):
        h = rms_norm(x, norm_mix[l])
        z = h @ w_in[l]
        z_a, z_b, z_cq, z_ckv_c, z_ckv_s, z_ckv_w, z_cg = jnp.split(z, split_at, axis=-1)
        out_a = spatial_gating(z_a, gmlp_ln_g[l], gmlp_ln_b[l], gmlp_w_s[l], gmlp_b_s[l])
        qkv_b = z_b.reshape(bsz, S, 3, B_HEADS, HEAD_DIM).transpose(2, 0, 3, 1, 4)
        out_b = dilated_attention(qkv_b[0], qkv_b[1], qkv_b[2])
        q_c = z_cq.reshape(bsz, S, C_KV_HEADS, C_GROUP, HEAD_DIM).transpose(0, 2, 3, 1, 4)

        def kv_heads(t):
            return t.reshape(bsz, S, 2, C_KV_HEADS, HEAD_DIM).transpose(2, 0, 3, 1, 4)

        out_c = nsa_attention(q_c, kv_heads(z_ckv_c), kv_heads(z_ckv_s), kv_heads(z_ckv_w), z_cg,
                              cmp_pos[l], cmp_k_w1[l], cmp_k_w2[l], cmp_v_w1[l], cmp_v_w2[l])
        x = x + jnp.concatenate([out_a, out_b, out_c], axis=-1) @ w_out[l]
        h = rms_norm(x, norm_xattn[l])
        m = rms_norm(mem, norm_mem[l])
        q = (h @ xattn_wq[l]).reshape(bsz, S, X_HEADS, HEAD_DIM)
        kv = (m @ xattn_wkv[l]).reshape(bsz, n_mem, 2, X_HEADS, HEAD_DIM)
        s = jnp.einsum('bshd,bmhd->bhsm', q, kv[:, :, 0]).astype(jnp.float32) * x_scale
        p = jax.nn.softmax(s, axis=-1).astype(x.dtype)
        o = jnp.einsum('bhsm,bmhd->bshd', p, kv[:, :, 1]).reshape(bsz, S, X_WIDTH)
        x = x + o @ xattn_wo[l]
        h = rms_norm(x, norm_mlp[l])
        x = x + jnp.square(jax.nn.relu(h @ w_up[l])) @ w_down[l]
    return rms_norm(x, final_norm)


GRID_W = 64
CTX_LEN = 256
HG_HEADS = 8
HG_DK = 128
HG_DV = 128
HG_WIDTH = HG_HEADS * HG_DV
HG_CHUNK = 32
ATT_HEADS = 8
ATT_KV_HEADS = 2
ATT_WIDTH = ATT_HEADS * HEAD_DIM
WINDOW = 128
ATT_BLOCK = 128
ROPE_THETA = 10000.0
D_MIX = HG_WIDTH + ATT_WIDTH
HG_COLS = 3 * HG_HEADS * HG_DK + 2 * HG_HEADS * HG_DV
ATT_COLS = (ATT_HEADS + 2 * ATT_KV_HEADS) * HEAD_DIM
IN_COLS = HG_COLS + ATT_COLS
D_FF_2 = ((8 * D_MODEL + 3 * 256 - 1) // (3 * 256)) * 256
N_MOD = 6
RMS_EPS = 1e-6
NEG_INF_2 = -1e30
LB_SLACK = 1.0


def rms_norm_2(x, g):
    xf = x.astype(jnp.float32)
    y = xf * lax.rsqrt(jnp.mean(xf * xf, axis=-1, keepdims=True) + RMS_EPS)
    return (y * g.astype(jnp.float32)).astype(x.dtype)

def modulate(h, shift, scale):
    return h * (1 + scale) + shift

def axial_rope(x, row, col):
    half = HEAD_DIM // 2
    nf = half // 2
    inv_freq = ROPE_THETA ** (-jnp.arange(nf, dtype=jnp.float32) / nf)
    extra = (1,) * (x.ndim - 3)

    def rotate(xa, pos):
        ang = pos.astype(jnp.float32)[:, None] * inv_freq
        cos = jnp.cos(ang).reshape((1, -1) + extra + (nf,))
        sin = jnp.sin(ang).reshape((1, -1) + extra + (nf,))
        x1 = xa[..., :nf].astype(jnp.float32)
        x2 = xa[..., nf:].astype(jnp.float32)
        return jnp.concatenate([x1 * cos - x2 * sin, x1 * sin + x2 * cos], axis=-1)

    out = jnp.concatenate([rotate(x[..., :half], row), rotate(x[..., half:], col)], axis=-1)
    return out.astype(x.dtype)

def chunked_gated_linear_scan(q, k, v, log_f, s0):
    B, H, T, DK = q.shape
    DV = v.shape[-1]
    N = T // HG_CHUNK
    q = q.reshape(B, H, N, HG_CHUNK, DK)
    k = k.reshape(B, H, N, HG_CHUNK, DK)
    v = v.reshape(B, H, N, HG_CHUNK, DV)
    b = jnp.cumsum(log_f.reshape(B, H, N, HG_CHUNK, DK), axis=3)
    b_last = b[:, :, :, -1:, :]
    q_dec = q * jnp.exp(b)
    k_inv = k * jnp.exp(-b)
    causal_in_chunk = jnp.tril(jnp.ones((HG_CHUNK, HG_CHUNK), dtype=bool))
    scores = jnp.einsum('bhnck,bhnsk->bhncs', q_dec, k_inv)
    scores = jnp.where(causal_in_chunk, scores, 0.0)
    o_intra = jnp.einsum('bhncs,bhnsv->bhncv', scores, v)
    kv_chunk = jnp.einsum('bhnsk,bhnsv->bhnkv', k * jnp.exp(b_last - b), v)
    decay = jnp.exp(b_last[:, :, :, 0, :])

    def step(s, inp):
        d, u = inp
        return d[..., None] * s + u, s

    s_final, s_starts = lax.scan(step, s0, (jnp.moveaxis(decay, 2, 0), jnp.moveaxis(kv_chunk, 2, 0)))
    s_starts = jnp.moveaxis(s_starts, 0, 2)
    o_inter = jnp.einsum('bhnck,bhnkv->bhncv', q_dec, s_starts)
    return (o_intra + o_inter).reshape(B, H, T, DV), s_final

def reverse_gated_linear_scan(q, k, v, log_f, s0):
    flip = lambda a: jnp.flip(a, axis=2)
    o, s = chunked_gated_linear_scan(flip(q), flip(k), flip(v), flip(log_f), s0)
    return flip(o), s

def hgrn2_mixer(p_lat, p_ctx, lb, norm_g, need_ctx_out):
    splits = [HG_HEADS * HG_DK, 2 * HG_HEADS * HG_DK, 3 * HG_HEADS * HG_DK,
              3 * HG_HEADS * HG_DK + HG_HEADS * HG_DV]

    def prep(p):
        B, T, _ = p.shape
        heads = lambda a: a.reshape(B, T, HG_HEADS, -1).transpose(0, 2, 1, 3).astype(jnp.float32)
        q, f_fwd, f_bwd, i, g = jnp.split(p, splits, axis=-1)
        q = jax.nn.silu(heads(q))
        gates = []
        for d, f_pre in enumerate((f_fwd, f_bwd)):
            lb_d = lb[d].reshape(HG_HEADS, 1, HG_DK)
            f = lb_d + (1.0 - lb_d) * jax.nn.sigmoid(heads(f_pre))
            gates.append((1.0 - f, jnp.log(f)))
        return q, heads(i), gates, g

    def readout(o, g):
        B, H, T, DV = o.shape
        o = rms_norm_2(o, norm_g).transpose(0, 2, 1, 3).reshape(B, T, H * DV)
        return (o * jax.nn.silu(g.astype(jnp.float32))).astype(g.dtype)

    qc, ic, (gc_f, gc_b), g_c = prep(p_ctx)
    ql, il, (gl_f, gl_b), g_l = prep(p_lat)
    B = p_lat.shape[0]
    zero = jnp.zeros((B, HG_HEADS, HG_DK, HG_DV), jnp.float32)
    oc_f, s_ctx_f = chunked_gated_linear_scan(qc, gc_f[0], ic, gc_f[1], zero)
    oc_b, s_ctx_b = reverse_gated_linear_scan(qc, gc_b[0], ic, gc_b[1], zero)
    ol_f, _ = chunked_gated_linear_scan(ql, gl_f[0], il, gl_f[1], s_ctx_f)
    ol_b, _ = reverse_gated_linear_scan(ql, gl_b[0], il, gl_b[1], s_ctx_b)
    lat_out = readout(ol_f + ol_b, g_l)
    ctx_out = readout(oc_f + oc_b, g_c) if need_ctx_out else None
    return lat_out, ctx_out

def window_attention(p_lat, p_ctx, q_g, k_g, sink, row, col, need_ctx_out):
    G = ATT_HEADS // ATT_KV_HEADS
    scale = HEAD_DIM ** -0.5

    def split_heads(p):
        B, T, _ = p.shape
        q, k, v = jnp.split(p, [ATT_HEADS * HEAD_DIM, (ATT_HEADS + ATT_KV_HEADS) * HEAD_DIM], axis=-1)
        q = rms_norm_2(q.reshape(B, T, ATT_KV_HEADS, G, HEAD_DIM), q_g)
        k = rms_norm_2(k.reshape(B, T, ATT_KV_HEADS, HEAD_DIM), k_g)
        return q, k, v.reshape(B, T, ATT_KV_HEADS, HEAD_DIM)

    ql, kl, vl = split_heads(p_lat)
    qc, kc, vc = split_heads(p_ctx)
    ql = axial_rope(ql, row, col)
    kl = axial_rope(kl, row, col)
    B, T = p_lat.shape[:2]
    L = p_ctx.shape[1]
    NB = T // ATT_BLOCK
    sink_f = sink.astype(jnp.float32).reshape(ATT_KV_HEADS, G, 1, 1)

    qb = ql.reshape(B, NB, ATT_BLOCK, ATT_KV_HEADS, G, HEAD_DIM)
    pad = ((0, 0), (ATT_BLOCK, ATT_BLOCK), (0, 0), (0, 0))
    kp = jnp.pad(kl, pad).reshape(B, NB + 2, ATT_BLOCK, ATT_KV_HEADS, HEAD_DIM)
    vp = jnp.pad(vl, pad).reshape(B, NB + 2, ATT_BLOCK, ATT_KV_HEADS, HEAD_DIM)
    k_band = jnp.concatenate([kp[:, :-2], kp[:, 1:-1], kp[:, 2:]], axis=2)
    v_band = jnp.concatenate([vp[:, :-2], vp[:, 1:-1], vp[:, 2:]], axis=2)
    s_band = jnp.einsum('bnqhgd,bnkhd->bhgnqk', qb, k_band).astype(jnp.float32) * scale
    s_ctx = jnp.einsum('bnqhgd,bkhd->bhgnqk', qb, kc).astype(jnp.float32) * scale
    qi = jnp.arange(ATT_BLOCK)[:, None]
    kj = jnp.arange(3 * ATT_BLOCK)[None, :]
    within = jnp.abs(kj - ATT_BLOCK - qi) <= WINDOW
    k_pos = (jnp.arange(NB)[:, None] - 1) * ATT_BLOCK + kj
    in_range = (k_pos >= 0) & (k_pos < T)
    mask = within[None, :, :] & in_range[:, None, :]
    s_band = jnp.where(mask, s_band, NEG_INF_2)
    sink_col = jnp.broadcast_to(sink_f[None, :, :, :, :, None], s_band.shape[:-1] + (1,))
    probs = jax.nn.softmax(jnp.concatenate([s_band, s_ctx, sink_col], axis=-1), axis=-1)
    p_band = probs[..., :3 * ATT_BLOCK].astype(vl.dtype)
    p_ctxk = probs[..., 3 * ATT_BLOCK:3 * ATT_BLOCK + L].astype(vc.dtype)
    o_lat = (jnp.einsum('bhgnqk,bnkhd->bnqhgd', p_band, v_band)
             + jnp.einsum('bhgnqk,bkhd->bnqhgd', p_ctxk, vc))
    lat_out = o_lat.reshape(B, T, ATT_WIDTH)

    ctx_out = None
    if need_ctx_out:
        sc = jnp.einsum('bqhgd,bkhd->bhgqk', qc, kc).astype(jnp.float32) * scale
        sink_c = jnp.broadcast_to(sink_f[None, :, :, :, :], sc.shape[:-1] + (1,))
        pc = jax.nn.softmax(jnp.concatenate([sc, sink_c], axis=-1), axis=-1)[..., :L]
        o_c = jnp.einsum('bhgqk,bkhd->bqhgd', pc.astype(vc.dtype), vc)
        ctx_out = o_c.reshape(B, L, ATT_WIDTH)
    return lat_out, ctx_out

def swiglu(h, w_gate_up, w_down):
    gate, up = jnp.split(h @ w_gate_up, 2, axis=-1)
    return (jax.nn.silu(gate) * up) @ w_down

def second_inputs(seed: int = 0) -> dict:
    key = jax.random.key(seed)
    ks = jax.random.split(key, 17)
    nrm = lambda k, shape, s: s * jax.random.normal(k, shape, jnp.float32)
    hg_lb = nrm(ks[9], (DEPTH + 1, 2, HG_HEADS * HG_DK), 0.1).at[DEPTH].add(LB_SLACK)
    return {
        "x": nrm(ks[0], (BATCH, SEQ, D_MODEL), 1.0),
        "c": nrm(ks[1], (BATCH, D_MODEL), 1.0),
        "ctx": nrm(ks[2], (BATCH, CTX_LEN, D_MODEL), 1.0),
        "c_ctx": nrm(ks[3], (D_MODEL,), 1.0),
        "w_mod": nrm(ks[4], (DEPTH, D_MODEL, N_MOD * D_MODEL), 0.5 * D_MODEL ** -0.5),
        "b_mod": nrm(ks[5], (DEPTH, N_MOD * D_MODEL), 0.01),
        "norm_mix_g": 1.0 + nrm(ks[6], (DEPTH, D_MODEL), 0.05),
        "norm_ffn_g": 1.0 + nrm(ks[7], (DEPTH, D_MODEL), 0.05),
        "w_in": nrm(ks[8], (DEPTH, D_MODEL, IN_COLS), D_MODEL ** -0.5),
        "hg_lb": hg_lb,
        "hg_norm_g": 1.0 + nrm(ks[10], (DEPTH, HG_DV), 0.05),
        "q_norm_g": 1.0 + nrm(ks[11], (DEPTH, HEAD_DIM), 0.05),
        "k_norm_g": 1.0 + nrm(ks[12], (DEPTH, HEAD_DIM), 0.05),
        "attn_sink": nrm(ks[13], (DEPTH, ATT_HEADS), 1.0),
        "w_out": nrm(ks[14], (DEPTH, D_MIX, D_MODEL), D_MIX ** -0.5),
        "w_gate_up": nrm(ks[15], (DEPTH, D_MODEL, 2 * D_FF_2), D_MODEL ** -0.5),
        "w_down": nrm(ks[16], (DEPTH, D_FF_2, D_MODEL), D_FF_2 ** -0.5),
    }

def second_block(x, c, ctx, c_ctx, w_mod, b_mod, norm_mix_g, norm_ffn_g, w_in, hg_lb,
              hg_norm_g, q_norm_g, k_norm_g, attn_sink, w_out, w_gate_up, w_down):
    T = x.shape[1]
    rows = T // GRID_W
    row = jnp.broadcast_to(jnp.arange(rows)[:, None], (rows, GRID_W)).reshape(-1)
    col = jnp.broadcast_to(jnp.arange(GRID_W)[None, :], (rows, GRID_W)).reshape(-1)
    lb_all = jnp.cumsum(jax.nn.softmax(hg_lb.astype(jnp.float32), axis=0), axis=0)
    y = ctx
    for l in range(DEPTH):
        need_ctx_out = l < DEPTH - 1
        sh_m, sc_m, gt_m, sh_f, sc_f, gt_f = [m[:, None, :] for m in
            jnp.split(jax.nn.silu(c) @ w_mod[l] + b_mod[l], N_MOD, axis=-1)]
        csh_m, csc_m, cgt_m, csh_f, csc_f, cgt_f = jnp.split(
            jax.nn.silu(c_ctx) @ w_mod[l] + b_mod[l], N_MOD, axis=-1)

        h_lat = modulate(rms_norm_2(x, norm_mix_g[l]), sh_m, sc_m)
        h_ctx = modulate(rms_norm_2(y, norm_mix_g[l]), csh_m, csc_m)
        p_lat = h_lat @ w_in[l]
        p_ctx = h_ctx @ w_in[l]
        hg_lat, hg_ctx = hgrn2_mixer(p_lat[..., :HG_COLS], p_ctx[..., :HG_COLS],
                                     lb_all[l], hg_norm_g[l], need_ctx_out)
        at_lat, at_ctx = window_attention(p_lat[..., HG_COLS:], p_ctx[..., HG_COLS:],
                                          q_norm_g[l], k_norm_g[l], attn_sink[l],
                                          row, col, need_ctx_out)
        x = x + gt_m * (jnp.concatenate([hg_lat, at_lat], axis=-1) @ w_out[l])

        x = x + gt_f * swiglu(modulate(rms_norm_2(x, norm_ffn_g[l]), sh_f, sc_f),
                              w_gate_up[l], w_down[l])

        if need_ctx_out:
            y = y + cgt_m * (jnp.concatenate([hg_ctx, at_ctx], axis=-1) @ w_out[l])
            y = y + cgt_f * swiglu(modulate(rms_norm_2(y, norm_ffn_g[l]), csh_f, csc_f),
                                   w_gate_up[l], w_down[l])
    return x


def setup_inputs(seed=0):
    out = dict(first_inputs(seed))
    for name, value in second_inputs(seed + 1).items():
        if name != "x":
            out[name + "_2"] = value
    return out


def reference(
    x, mem, norm_mix, w_in, gmlp_ln_g, gmlp_ln_b, gmlp_w_s, gmlp_b_s, cmp_pos, cmp_k_w1,
    cmp_k_w2, cmp_v_w1, cmp_v_w2, w_out, norm_xattn, norm_mem, xattn_wq, xattn_wkv, xattn_wo,
    norm_mlp, w_up, w_down, final_norm, c_2, ctx_2, c_ctx_2, w_mod_2, b_mod_2, norm_mix_g_2,
    norm_ffn_g_2, w_in_2, hg_lb_2, hg_norm_g_2, q_norm_g_2, k_norm_g_2, attn_sink_2, w_out_2,
    w_gate_up_2, w_down_2,
):
    x = first_block(
        x, mem, norm_mix, w_in, gmlp_ln_g, gmlp_ln_b, gmlp_w_s, gmlp_b_s, cmp_pos, cmp_k_w1,
        cmp_k_w2, cmp_v_w1, cmp_v_w2, w_out, norm_xattn, norm_mem, xattn_wq, xattn_wkv,
        xattn_wo, norm_mlp, w_up, w_down, final_norm,
    )
    return second_block(
        x, c_2, ctx_2, c_ctx_2, w_mod_2, b_mod_2, norm_mix_g_2, norm_ffn_g_2, w_in_2, hg_lb_2,
        hg_norm_g_2, q_norm_g_2, k_norm_g_2, attn_sink_2, w_out_2, w_gate_up_2, w_down_2,
    )


_drawn_inputs = setup_inputs


def setup_inputs(seed=0):
    import zlib

    import numpy as np

    out = dict(_drawn_inputs(seed))
    spreads = {}
    factors = {'norm_mix': 8.0,
     'gmlp_ln_g': 8.0,
     'gmlp_ln_b': 8.0,
     'gmlp_b_s': 8.0,
     'cmp_pos': 8.0,
     'norm_xattn': 8.0,
     'norm_mem': 8.0,
     'norm_mlp': 4.803,
     'final_norm': 2.765,
     'ctx_2': 4.134,
     'b_mod_2': 5.554,
     'norm_mix_g_2': 5.855,
     'norm_ffn_g_2': 3.963,
     'hg_norm_g_2': 7.494,
     'q_norm_g_2': 8.0,
     'k_norm_g_2': 8.0,
     'attn_sink_2': 8.0}
    for name, (base, spread) in spreads.items():
        noise = np.random.default_rng([zlib.crc32(name.encode()), seed]).standard_normal(out[name].shape)
        drawn = base * np.exp(spread * noise) if base else spread * noise
        out[name] = jnp.asarray(drawn.astype(out[name].dtype))
    for name, factor in factors.items():
        out[name] = (out[name] * factor).astype(out[name].dtype)
    return out
```

```python
import numpy as np
import concourse.bass as bass
from concourse import mybir

F = mybir.dt.float32
R = mybir.dt.float32r
ALU = mybir.AluOpType
ACT = mybir.ActivationFunctionType
AX = mybir.AxisListType.X

D = 2048
S = 256
SC = 128.0 ** -0.5
BIG = 3.0e38
EPS = 1e-6
NCH = 2
NRAW, NHI, LOOK = 6, 4, 3
FF2 = 5632

MSK, IDN, ONE, LMK, TRL, CMK, RVD, ROC, ROS, HGM, NCONST = (
    0, 896, 1024, 1152, 1408, 1536, 1566, 1568, 1824, 2080, 2852)


def constants():
    c = np.zeros((128, NCONST), np.float32)
    i = np.arange(128)[:, None]
    j = np.arange(128)[None, :]
    neg = np.float32(-1e30)
    c[:, 0:128] = np.where(j >= i, 0, neg)
    c[:, 512:640] = np.where(j <= i, 0, neg)
    c[:, IDN:IDN + 128] = i == j
    c[:, ONE:ONE + 128] = 1.0
    d = 128 + i - np.arange(256)[None, :]
    n = ((d >= 0) & (d <= 128)).astype(int) + ((d >= 0) & (d % 4 == 0)) + ((d >= 0) & (d % 16 == 0))
    c[:, LMK:LMK + 256] = np.where(n > 0, np.log(np.maximum(n, 1)) / SC, neg)
    c[:, TRL:TRL + 128] = i <= j
    for tb in range(2):
        e = np.arange(15)[None, :] * 16 + 31
        ok = e <= i + 128 * tb
        c[:, CMK + 15 * tb:CMK + 15 * tb + 15] = np.where(ok, 0, neg)
        c[:, RVD + tb:RVD + tb + 1] = ok.any(1, keepdims=True)
        t = np.arange(128) + 128 * tb
        f = np.float32(10000.0) ** (-np.arange(32, dtype=np.float32) / np.float32(32))
        for half, pos in ((0, t // 64), (1, t % 64)):
            a = pos.astype(np.float32)[:, None] * f[None, :].astype(np.float32)
            o = 128 * tb + 64 * half
            c[:, ROC + o:ROC + o + 32] = np.cos(a)
            c[:, ROC + o + 32:ROC + o + 64] = np.cos(a)
            c[:, ROS + o:ROS + o + 32] = -np.sin(a)
            c[:, ROS + o + 32:ROS + o + 64] = np.sin(a)
    same = (i // 32) == (j // 32)
    for k, m in enumerate(((i <= j) & same, (i >= j) & same, (i > j) & same, (i < j) & same, i > j, i < j)):
        c[:, HGM + 128 * k:HGM + 128 * k + 128] = m
    c[:, HGM + 768:HGM + 772] = (i // 32) == np.arange(4)[None, :]
    return c


class Queue:

    def __init__(self, sem):
        self.sem, self.n, self.items = sem, 0, []

    def __call__(self, fn, *waits, inc=True):
        self.items.append((list(flat(waits)), fn, self.sem if inc else None, 1))
        if inc:
            self.n += 1
            return (self.sem, self.n)
        return None

    def replay(self, eng):
        seen = {}
        for waits, fn, sem, by in self.items:
            need = {}
            for w in waits:
                need[w[0]] = max(need.get(w[0], 0), w[1])
            for s, v in need.items():
                if seen.get(s, 0) < v:
                    eng.wait_ge(s, v)
                    seen[s] = v
            if fn is not None:
                ins = fn(eng)
                if sem is not None:
                    ins.then_inc(sem, by)


def flat(ws):
    for w in ws:
        if w is None:
            continue
        if isinstance(w, list):
            yield from flat(w)
        else:
            yield w


class Operand:

    def __init__(self, h, l):
        self.h, self.l = h, l
        self.tok = [[] for _ in range(16)]
        self.read = []


class Ring:
    def __init__(self, items):
        self.items = list(items)
        self.free = [[] for _ in items]
        self.order = list(range(len(items)))

    def ready(self):
        return len(self.order) > 0

    def take(self):
        k = self.order.pop(0)
        return k, self.items[k], self.free[k]

    def give(self, k, toks):
        self.free[k] = toks
        self.order.append(k)


def program(nc, a):
    base = [16512]
    top = nc.sbuf_usable_end

    def region(n):
        at = base[0]
        base[0] += n
        assert base[0] <= top, (base[0], top)
        return at

    def sb(name, at, shape, dt=F):
        return nc.alloc_sbuf_tensor_at(name, [128] + list(shape), dt, offset=at)

    rX = region(16384)
    rT1 = region(32768)
    rT2 = region(32768)
    rW = region(4096 * (NRAW + NHI))
    rZ = region(38912)
    rS = region(16384)
    rM = region(8192)
    rG = region(8192)
    rA = region(4096)
    rC = region(4608)
    rY = region(5120)
    rQ = region(4096)

    x = sb("x", rX, [2, D])
    T = {}
    for nm, at in (("1", rT1), ("2", rT2), ("3", rZ)):
        T[nm] = (sb("th" + nm, at, [16, S], R), sb("tl" + nm, at + 16384, [16, S], R))
    raws = [sb(f"raw{i}", rW + 4096 * i, [1024]) for i in range(NRAW)]
    los = [sb(f"wlo{i}", rW + 4096 * i, [1024], R) for i in range(NRAW)]
    his = [sb(f"whi{i}", rW + 4096 * (NRAW + i), [1024], R) for i in range(NHI)]
    stg = [sb(f"stg{i}", rG + 4096 * i, [2, 512]) for i in range(2)]
    acc = [sb(f"acc{i}", rA + 2048 * i, [512]) for i in range(2)]
    mskt = sb("mskt", rC, [896])
    ident = sb("ident", rC + 3584, [128])
    ones = sb("ones", rC + 4096, [128])
    z0 = rZ
    bq = sb("bq", z0, [4, S])
    bk = sb("bk", z0 + 4096, [4, S])
    bv = sb("bv", z0 + 8192, [2, 512])
    cq = sb("cq", z0 + 12288, [8, S])
    cc = sb("cc", z0 + 20480, [4, S])
    ckT = [sb(f"ckT{i}", z0 + 24576 + 4096 * i, [2, S]) for i in range(2)]
    cv = [sb(f"cv{i}", z0 + 26624 + 4096 * i, [2, 256]) for i in range(2)]
    sv = sb("sv", z0 + 32768, [2, 512])
    memx = sb("memx", z0, [2, D])
    xn = sb("xn", rS, [D])
    yb = [sb(f"yb{i}", rS + 8192 + 2048 * i, [512]) for i in range(2)]
    cb = sb("cb", rS, [2, 32, 30])
    Eb = [sb(f"Eb{i}", rS + 2048 * i, [512]) for i in range(3)]
    PTb = [sb(f"PTb{i}", rS + 6144 + 4096 * i, [4, S]) for i in range(2)]
    PCb = [sb(f"PCb{i}", rS + 14336 + 1024 * i, [S]) for i in range(2)]
    mk = sb("mk", rM, [4, S])
    mv = sb("mv", rM + 4096, [2, 512])
    gt = sb("gt", rM, [D])
    lng = sb("lng", rY, [512])
    lnb = sb("lnb", rY + 2048, [512])
    lmk = sb("lmk", rY + 4096, [256])
    ropc = sb("ropc", rY, [2, 128])
    rops = sb("rops", rY + 1024, [2, 128])
    hgm = sb("hgm", rY + 2048, [6, 128])
    q0 = [rQ]

    def small(name, shape):
        n = 4
        for s in shape:
            n *= s
        at = q0[0]
        q0[0] += (n + 31) // 32 * 32
        assert q0[0] <= rQ + 4096 + (top - base[0]), name
        return sb(name, at, shape)

    cols = small("cols", [96])
    cols2 = small("cols2", [69])
    silc = small("silc", [32])
    mod = small("mod", [64])
    modx = small("modx", [32])
    gmod = small("gmod", [2, 16])
    cg = small("cg", [2, 24])
    pc = small("pc", [2, 8, 15])
    cmk = small("cmk", [32])
    hT = small("hT", [2, 32])
    kcT = small("kcT", [32])
    ssp = small("ssp", [2, 4])
    st = small("st", [16])
    sm = small("sm", [96])
    dec = small("dec", [2, 8])
    sink = small("sink", [8])
    ln4 = small("ln4", [8])
    chm = small("chm", [4])
    b2 = rZ
    hK = sb("hK", b2, [2, 512])
    hE1 = [sb(f"hE1{i}", b2 + 4096 + 1024 * i, [S]) for i in range(2)]
    hE2 = [sb(f"hE2{i}", b2 + 6144 + 1024 * i, [S]) for i in range(2)]
    hQ = sb("hQ", b2 + 8192, [4, S])
    hV = sb("hV", b2 + 12288, [2, 512])
    hO = sb("hO", b2 + 16384, [4, S])
    lb = sb("lb", b2 + 20480, [2, 512])
    hST = [sb(f"hST{i}", b2 + 24576 + 1024 * i, [2, 128]) for i in range(2)]
    S0 = sb("S0", b2 + 26624, [16, 128])
    xkT = sb("xkT", b2 + 34816, [2, S])
    xv = sb("xv", b2 + 36864, [2, 256])
    hA = sb("hA", rS, [2, 512])
    hE = sb("hE", rS + 4096, [2, 512])
    hS = [sb("hS0", rS + 8192, [8, 128])]
    hM = [sb(f"hM{i}", rS + 12288 + 2048 * i, [4, 128]) for i in range(2)]
    lkT = sb("lkT", b2, [2, S])
    lv = sb("lv", b2 + 2048, [2, 256])
    lq = sb("lq", b2 + 4096, [8, S])
    rt = sb("rt", b2 + 12288, [2, 512])
    rt2 = sb("rt2", b2 + 16384, [2, 512])
    qkg = sb("qkg", b2 + 20480, [2, 128])
    wk2 = sb("wk2", z0 + 36864, [2, 128])
    vcs = sb("vcs", z0 + 37888, [2, 128])
    wsT = sb("wsT", z0 + 16384, [4, 128])
    wsr = sb("wsr", z0 + 18432, [4, 128])
    trl = sb("trl", z0 + 20480, [128])
    rows = sb("rows", rG, [128])
    rows2 = sb("rows2", rG + 512, [128])

    ps = [nc.alloc_psum_tensor(f"ps{i}", [128, 512], F) for i in range(8)]

    def sem(name):
        return nc.alloc_semaphore(name)

    s_pe, s_act, s_dve, s_pool = sem("s_pe"), sem("s_act"), sem("s_dve"), sem("s_pool")
    s_raw = [sem(f"s_raw{i}") for i in range(NRAW)]
    misc = [sem(f"s_m{i}") for i in range(60)]
    s_out = sem("s_out")

    def emit(plan):
        PE, AC, DV, PO = Queue(s_pe), Queue(s_act), Queue(s_dve), Queue(s_pool)
        SP = Queue(None)
        nm = [0]

        def load(dst, src, *waits, q=None):
            s = misc[nm[0]]
            nm[0] += 1
            (q or SP).items.append((list(flat(waits)), lambda e: e.dma_start(dst, src), s, 16))
            return (s, 16)

        rec = []
        stream = {"next": 0, "dma": 0, "prep": 0, "g": 0, "gn": 0}
        raw_free = {}
        hi_free = {}
        ready = {}

        def issue_dma():
            while plan is not None and stream["dma"] < len(plan):
                j = stream["dma"]
                if j >= NRAW and (j - NRAW) not in raw_free:
                    break
                kind, src, shape = plan[j]
                dst = view(raws[j % NRAW], shape)
                SP.items.append((list(flat([raw_free.get(j - NRAW)])), lambda e, dst=dst, src=src: e.dma_start(dst, src),
                                 s_raw[j % NRAW], 16))
                stream["dma"] += 1

        def view(t, shape):
            n = shape[0] * shape[1]
            return t[:, 0:n].rearrange("p (a b) -> p a b", a=shape[0])

        def prepare():
            issue_dma()
            while plan is not None and stream["prep"] < stream["dma"]:
                j = stream["prep"]
                kind, src, shape = plan[j]
                landed = (s_raw[j % NRAW], 16 * (j // NRAW + 1))
                if kind == "m":
                    if not MD["todo"]:
                        break
                    mod_step()
                    issue_dma()
                    continue
                if kind == "r":
                    ready[j] = (landed, None, None, None)
                    stream["prep"] += 1
                    continue
                g = stream["g"]
                if g > stream["gn"] + LOOK:
                    break
                assert g < NHI or g - NHI in hi_free
                used = hi_free.get(g - NHI)
                stream["g"] += 1
                n = shape[0] * shape[1]
                rw, hi, lo = raws[j % NRAW][:, 0:n], his[g % NHI][:, 0:n], los[j % NRAW][:, 0:n]
                th = AC(lambda e, rw=rw, hi=hi: e.activation(hi, rw, ACT.Copy), landed, used)
                tl = DV(lambda e, rw=rw, hi=hi, lo=lo: e.tensor_tensor(lo, rw, hi.bitcast(F), ALU.subtract),
                        landed, th)
                ready[j] = (landed, g, [th, tl], (view(his[g % NHI], shape), view(los[j % NRAW], shape)))
                stream["prep"] += 1

        def chunk(kind, src, shape):
            if plan is None:
                j = len(rec)
                rec.append((kind, src, shape))
                return j, ((s_raw[0], 0), j, None, (view(his[0], shape), view(los[0], shape)))
            if kind == "m":
                j = stream["prep"]
                assert plan[j][0] == kind
                stream["prep"] += 1
                return j, ((s_raw[j % NRAW], 16 * (j // NRAW + 1)), None, None, None)
            while plan[stream["next"]][0] == "m":
                stream["next"] += 1
            j = stream["next"]
            assert plan[j][0] == kind and plan[j][2] == shape
            prepare()
            assert stream["prep"] > j
            stream["next"] += 1
            return j, ready[j]

        lanes = {"small": [], "big": [], "mod": []}

        def step(name):
            q = lanes[name]
            if q:
                try:
                    next(q[0])
                except StopIteration:
                    q.pop(0)

        def tick():
            step("small")
            step("big")
            step("mod")
            mods_tick()

        def drain(name):
            while lanes[name]:
                step(name)

        def spawn(name, gen):
            lanes[name].append(gen)

        pairs = Ring([(ps[0], ps[1]), (ps[2], ps[3])])
        eb = Ring([ps[4]])
        bb = Ring([ps[5], ps[6], ps[7]])

        stgs = Ring(stg)

        def gemm(op, w, row0, col0, n, kts, epi, lane="small"):
            while not pairs.ready():
                step("small")
                if not lanes["small"]:
                    step("big")
            k, (p0, p1), freed = pairs.take()
            i, step_n = 0, (NCH if n == 512 else len(kts))
            while i < len(kts):
                m = min(step_n, len(kts) - i)
                r = row0 + 128 * i
                src = w[r:r + 128 * m, col0:col0 + n].rearrange("(a p) n -> p a n", p=128)
                j, (_, g, toks, (wh, wl)) = chunk("g", src, (m, n))
                for c in range(m):
                    kt = kts[i + c]
                    first, last = i + c == 0, i + c == len(kts) - 1
                    for tb, p in ((0, p0), (1, p1)):
                        xh = op.h[:, kt, 128 * tb:128 * tb + 128]
                        xl = op.l[:, kt, 128 * tb:128 * tb + 128]
                        trio = ((xh, wh), (xh, wl), (xl, wh))
                        for z, (s, v) in enumerate(trio):
                            end = c == m - 1 and tb == 1 and z == 2
                            t = PE(lambda e, p=p, s=s, v=v, c=c, f=first and z == 0, l=last and z == 2:
                                   e.matmul(p[:, 0:n], s, v[:, c, :], start=f, stop=l),
                                   toks, op.tok[kt], freed if first else None, inc=end)
                hi_free[g] = t
                raw_free[j] = t
                stream["gn"] += 1
                i += m
                tick()
            op.read = [t]

            def release(toks):
                pairs.give(k, toks)
            epi((p0, p1), t, release)
            return t

        def act(out, in_, f, *w, **kw):
            return AC(lambda e: e.activation(out, in_, f, **kw), *w)

        def tt(out, i0, i1, op, *w):
            return DV(lambda e: e.tensor_tensor(out, i0, i1, op), *w)

        def ts(out, i0, s1, s2, o0, o1, *w):
            if o1 is None:
                return DV(lambda e: e.tensor_scalar(out, i0, s1, None, o0), *w)
            return DV(lambda e: e.tensor_scalar(out, i0, s1, s2, o0, o1), *w)

        def copy(out, in_, *w):
            return DV(lambda e: e.tensor_copy(out, in_), *w)

        def recip(out, in_, *w):
            return DV(lambda e: e.reciprocal(out, in_), *w)

        def transpose(out, in_, *w, inc=True, kp=128):
            return PE(lambda e: e.transpose(out, in_, ident[0:kp, 0:kp]), *w, inc=inc)

        def mm(out, l, r, first, last, *w, inc=False):
            return PE(lambda e: e.matmul(out, l, r, start=first, stop=last, skip_group_check=True), *w, inc=inc)

        def split(op, kts, c0, c1, src, *w):
            h, l = op.h[:, kts[0]:kts[-1] + 1, c0:c1], op.l[:, kts[0]:kts[-1] + 1, c0:c1]
            t1 = act(h, src, ACT.Copy, *w)
            t2 = tt(l, src, h.bitcast(F), ALU.subtract, t1, *w)
            for kt in kts:
                op.tok[kt] = op.tok[kt] + [t1, t2]
            return [t1, t2]

        def operand(nm, used):
            op = Operand(*T[nm])
            op.used = used
            return op

        def bc(ap, n):
            return ap.unsqueeze(2).broadcast_to([128, ap.shape[1], n])

        cd = a["consts"]
        t_c = [load(mskt[:, :], cd[:, 0:896]), load(ident[:, :], cd[:, IDN:IDN + 128]),
               load(ones[:, :], cd[:, ONE:ONE + 128])]
        t_x0 = load(memx[:, :, :], a["mem"][0].rearrange("(t p) d -> p t d", p=128))
        t_r = [load(rows[16 * i:16 * i + 16, :], a[n].rearrange("o (a p) -> (o a) p", p=128))
               for i, n in enumerate(("norm_mix", "norm_xattn", "norm_mem", "norm_mlp", "norm_mix_g_2", "norm_ffn_g_2"))]
        t_r2 = [load(rows2[0:16, :], a["c_2"].rearrange("o (a p) -> (o a) p", p=128)),
                load(rows2[16:32, :], a["c_ctx_2"].rearrange("(a p) -> a p", p=128)),
                load(rows2[32:36, :], a["gmlp_b_s"][0]),
                load(rows2[36:37, :], a["hg_norm_g_2"]),
                load(rows2[37:69, :], a["cmp_pos"][0])]
        t_x = load(x[:, :, :], a["x"][0].rearrange("(t p) d -> p t d", p=128))
        t_cst = [load(lmk[:, :], cd[:, LMK:LMK + 256]), load(trl[:, :], cd[:, TRL:TRL + 128]),
                 load(cmk[:, :], cd[:, CMK:CMK + 32])]
        t_ln = [load(lng[:, :], a["gmlp_ln_g"].broadcast_to([128, 512])),
                load(lnb[:, :], a["gmlp_ln_b"].broadcast_to([128, 512]))]
        t_ws = load(wsr[:, :, :], a["gmlp_w_s"][0].rearrange("g t s -> t g s"))
        t_w2 = [load(wk2[:, 0, :], a["cmp_k_w2"][0]), load(wk2[:, 1, :], a["cmp_v_w2"][0])]
        t_sink = load(sink[:, :], a["attn_sink_2"].broadcast_to([128, 8]))

        k, e0, _ = eb.take()
        transpose(e0[:, 0:96], rows[0:96, :], t_c, t_r, kp=96, inc=False)
        t = transpose(e0[:, 128:197], rows2[0:69, :], t_r2, kp=69)
        t_cols = copy(cols[:, :], e0[:, 0:96], t)
        t_cols2 = copy(cols2[:, :], e0[:, 128:197], t)
        eb.give(k, [t_cols, t_cols2])
        stgs.free = [[t], [t]]
        t_sil = act(silc[:, :], cols2[:, 0:32], ACT.Silu, t_cols2)
        gain = {n: cols[:, 16 * i:16 * i + 16] for i, n in enumerate(("mix", "xa", "mem", "mlp", "mix2", "ffn2"))}
        bsT, hgn, posT = cols2[:, 32:36], cols2[:, 36:37], cols2[:, 37:69]

        w_mod, b_mod = a["w_mod_2"][0], a["b_mod_2"]
        MD = {"todo": [], "credit": 0.0, "rate": 0.0, "acc": [None, None], "done": [], "gt": [], "xdone": [], "cur": None}

        def mod_step():
            j, kc, dest = MD["todo"].pop(0)
            both = j < 8
            if kc == 0:
                used = [0, 1] if both else [j % 2]
                if any(isinstance(MD["acc"][v], tuple) and MD["acc"][v][0] == "late" for v in used):
                    drain_mod_sums()
                MD["cur"] = [(v, PO(lambda e, v=v: e.memset(acc[v][:, :], 0.0), MD["acc"][v])) for v in used]
            src = w_mod[256 * kc:256 * kc + 256, 512 * j:512 * j + 512].rearrange("(a p) n -> p a n", p=128)
            jj, (landed, _, _, _) = chunk("m", src, (NCH, 512))
            rv = view(raws[jj % NRAW], (NCH, 512))
            for c in range(NCH):
                nxt = []
                for i, (v, t) in enumerate(MD["cur"]):
                    col = 16 * i + NCH * kc + c
                    sc = silc[:, col:col + 1]
                    nxt.append((v, DV(lambda e, v=v, c=c, sc=sc, rv=rv: e.scalar_tensor_tensor(
                        out=acc[v][:, :], in0=rv[:, c, :], scalar=sc, in1=acc[v][:, :],
                        op0=ALU.mult, op1=ALU.add), landed, t, t_sil)))
                MD["cur"] = nxt
            raw_free[jj] = [t for _, t in MD["cur"]]
            if kc == 7:
                spawn("mod", mod_sum(j, dest, MD["cur"]))
                for v, _ in MD["cur"]:
                    MD["acc"][v] = ("late", j)

        def drain_mod_sums():
            while lanes["mod"]:
                if not eb.ready():
                    step("small")
                step("mod")

        def mod_sum(j, dest, cur):
            while not eb.ready():
                yield
            k, e, fr = eb.take()
            if dest == "col":
                for i, (v, ta) in enumerate(cur):
                    for q in range(4):
                        t = mm(e[:, 4 * i + q:4 * i + q + 1], acc[v][:, 128 * q:128 * q + 128], ones[:, 0:1],
                               True, True, fr, ta, inc=(i == len(cur) - 1 and q == 3))
                jc = j if j < 8 else j - 4
                t1 = tt(mod[:, 4 * jc:4 * jc + 4], e[:, 0:4], bmc[:, 4 * j:4 * j + 4], ALU.add, t, t_bm)
                MD["done"].append(t1)
                outs = [t1]
                if len(cur) > 1:
                    t2 = tt(modx[:, 4 * j:4 * j + 4], e[:, 4:8], bmc[:, 4 * j:4 * j + 4], ALU.add, t, t_bm)
                    MD["xdone"].append(t2)
                    outs.append(t2)
            else:
                g = j % 4
                v, ta = cur[0]
                t = mm(e[:, :], ones[:, :], acc[v][:, :], True, True, fr, ta, inc=True)
                outs = [tt(gt[:, 512 * g:512 * g + 512], e[:, :], gt[:, 512 * g:512 * g + 512], ALU.add, t, MD["gtb"])]
                MD["gt"] += outs
            eb.give(k, outs)
            for v, _ in cur:
                MD["acc"][v] = t

        def mods_tick():
            if plan is not None or not MD["todo"]:
                return
            MD["credit"] += MD["rate"]
            while MD["credit"] >= 1 and MD["todo"]:
                MD["credit"] -= 1
                mod_step()

        def mods_start(j0, j1, dest, rate):
            mods_finish()
            MD["todo"] += [(j, kc, dest) for j in range(j0, j1) for kc in range(8)]
            MD["rate"], MD["credit"] = rate, 0.0

        def mods_finish():
            while MD["todo"]:
                n = len(MD["todo"])
                if plan is None:
                    mod_step()
                else:
                    prepare()
                assert len(MD["todo"]) < n
            drain_mod_sums()

        t_b0 = load(yb_rows(0), b_mod.rearrange("o (a p) -> (o a) p", p=128), t_cols)
        k, e0, fr = eb.take()
        t = transpose(e0[:, 0:96], yb_rows(0), fr, t_b0, kp=96)
        t_bm = copy(bmc[:, :], e0[:, 0:96], t)
        eb.give(k, [t_bm])
        stgs.free = [[t], [t]]

        def rstd_of(ss, n, out, *w):
            t1 = ts(out, ss, 1.0 / n, EPS, ALU.mult, ALU.add, *w)
            t2 = act(out, out, ACT.Sqrt, t1)
            return recip(out, out, t2)

        XN = {"free": [], "yb": [[], []], "n": 0}

        def turn(src, srct, rs, op, g, sh, gtok, used):
            def run():
                for tb in range(2):
                    t_n = ts(xn[:, :], src[:, tb, :], rs[tb][0], None, ALU.mult, None, srct, rs[tb][1], XN["free"])
                    for q in range(4):
                        while not eb.ready():
                            yield
                        k, e, fr = eb.take()
                        for i in range(4):
                            t = transpose(e[:, 128 * i:128 * i + 128], xn[:, 512 * q + 128 * i:512 * q + 128 * i + 128],
                                          t_n, fr, inc=(i == 3))
                        XN["free"] = [t]
                        u = XN["n"] % 2
                        XN["n"] += 1
                        ev = e[:, :].rearrange("p (a b) -> p a b", a=4)
                        yv = yb[u][:, :].rearrange("p (a b) -> p a b", a=4)
                        t1 = tt(yv, ev, bc(g[:, 4 * q:4 * q + 4], 128), ALU.mult, t, gtok, XN["yb"][u])
                        eb.give(k, [t1])
                        if sh is not None:
                            t1 = tt(yv, yv, bc(sh[:, 4 * q:4 * q + 4], 128), ALU.add, t1, gtok)
                        XN["yb"][u] = split(op, list(range(4 * q, 4 * q + 4)), 128 * tb, 128 * tb + 128, yv, t1, used)
                        yield
            return run()

        def stats(src, tok, dst):
            out = []
            for tb in range(2):
                t1 = act(xn[:, :], src[:, tb, :], ACT.Square, tok, XN["free"], accum_out=dst[:, tb:tb + 1])
                XN["free"] = [t1]
                out.append((dst[:, tb:tb + 1], rstd_of(dst[:, tb:tb + 1], D, dst[:, tb:tb + 1], t1)))
            return out

        def sums(dst, toks):
            out = []
            for tb in range(2):
                t1 = DV(lambda e, tb=tb: e.tensor_reduce(dst[:, tb:tb + 1], ssp[:, tb, :], AX, ALU.add), toks)
                out.append((dst[:, tb:tb + 1], rstd_of(dst[:, tb:tb + 1], D, dst[:, tb:tb + 1], t1)))
            return out

        def to_heads(dst, h0, f=ACT.Copy, used=(), done=None, nh=4, pre=None):
            def epi(p, t, release):
                def run():
                    while not stgs.ready():
                        yield
                    k, sg, fr = stgs.take()
                    w = 128 * nh
                    t0 = act(sg[:, 0, 0:w], p[0][:, 0:w], ACT.Copy, t, fr)
                    t1 = copy(sg[:, 1, 0:w], p[1][:, 0:w], t, fr)
                    release([t0, t1])
                    yield
                    out = []
                    for i in range(0, nh, 2):
                        while not eb.ready():
                            yield
                        kb, e, fb = eb.take()
                        for h in range(2):
                            for tb in range(2):
                                t2 = transpose(e[:, 256 * h + 128 * tb:256 * h + 128 * tb + 128],
                                               sg[:, tb, 128 * (i + h):128 * (i + h) + 128], t0, t1, fb,
                                               inc=(h == 1 and tb == 1))
                        t3 = act(dst[:, h0 + i:h0 + i + 2, :], e[:, :].rearrange("p (a b) -> p a b", a=2), f, t2, list(used))
                        eb.give(kb, [t3])
                        out.append(t3)
                        yield
                    stgs.give(k, [t2])
                    if done is not None:
                        done.extend(out)
                spawn("small", run())
            return epi

        def to_rows(dst, c0, n, s0, f, used, done):
            def epi(p, t, release):
                o = [act(dst[:, tb, c0:c0 + n], p[tb][:, s0:s0 + n], f, t, list(used)) for tb in range(2)]
                done.extend(o)
                release(o)
            return epi

        def two(e1, e2):
            def epi(p, t, release):
                got = []

                def one(toks):
                    got.append(toks)
                    if len(got) == 2:
                        release(got[0] + got[1])
                e2(p, t, one)
                e1(p, [t, got[0]], one)
            return epi

        RES = {"tok": [[t_x] for _ in range(8)], "ss": []}

        def residual(n, last, scale=None, out=None):
            def epi(p, t, release):
                o = []
                for tb in range(2):
                    xs = x[:, tb, 512 * n:512 * n + 512]
                    i = 2 * n + tb
                    if scale is None:
                        t1 = tt(xs, p[tb][:, :], xs, ALU.add, t, RES["tok"][i])
                        o.append(t1)
                    else:
                        k, sg, fr = stgs.take()
                        t0 = tt(sg[:, 0, :], p[tb][:, :], scale[:, 512 * n:512 * n + 512], ALU.mult, t, fr, MD["gt"])
                        o.append(t0)
                        t1 = tt(xs, sg[:, 0, :], xs, ALU.add, t0, RES["tok"][i])
                        stgs.give(k, [t1])
                    RES["tok"][i] = [t1]
                    if last:
                        t2 = act(yb[tb][:, :], xs, ACT.Square, t1, XN["yb"][tb], accum_out=ssp[:, tb, n:n + 1])
                        XN["yb"][tb] = [t2]
                        RES["ss"].append(t2)
                        RES["tok"][i] = [t1, t2]
                    if out is not None:
                        SP.items.append(([t1], lambda e, tb=tb, xs=xs: e.dma_start(
                            out[0, 128 * tb:128 * tb + 128, 512 * n:512 * n + 512], xs), s_out, 16))
                release(o)
            return epi

        def attention(nh, q, parts, op, kt0, used, qtok, post=None, snk=None, extra=None, fac=None):
            ER = Ring(Eb)
            PR = Ring(PTb)
            CR = Ring(PCb)
            for r in (ER, PR, CR):
                r.free = [list(used["scr"]) for _ in r.items]
            st8 = {"sm": 0}
            heads = {}
            smfree = [None] * 8

            def s1(u):
                h, tb = u["h"], u["tb"]
                u["bk"], bank, fr = bb.take()
                u["bank"] = bank
                last = [(p, z) for p in parts for z in p["k"](h, tb)]
                for i, (p, (kap, col)) in enumerate(last):
                    n = kap.shape[1]
                    u["t"] = mm(bank[:, col:col + n], q(h, tb), kap, True, True, fr, qtok, p["tok"],
                                inc=(i == len(last) - 1))

            def s2(u):
                h, tb = u["h"], u["tb"]
                i = (2 * h + tb) % 8
                sb8 = sm[:, 12 * i:12 * i + 12]
                u["s"] = sb8
                u["e"], E, fr = ER.take()
                u["E"] = E
                tks = []
                for j, p in enumerate(parts):
                    o, n = p["off"], p["n"](tb)
                    t = DV(lambda e, o=o, n=n, p=p, j=j, E=E, bank=u["bank"]: e.tensor_tensor_reduce(
                        E[:, o:o + n], bank[:, o:o + n], p["mask"](tb), -SC, BIG, ALU.add, ALU.min,
                        sb8[:, j:j + 1]), u["t"], fr, smfree[i])
                    tks.append(t)
                bb.give(u["bk"], tks)
                ex = []
                if snk is not None:
                    t = DV(lambda e: e.tensor_tensor(sb8[:, 0:1], sb8[:, 0:1], snk[1][:, h:h + 1], ALU.min), tks[0], snk[2])
                    tks[0] = t
                    ex.append(act(sb8[:, 8:9], snk[0][:, h:h + 1], ACT.Exp, t, bias=sb8[:, 0:1]))
                out = []
                for j, p in enumerate(parts):
                    o, n = p["off"], p["n"](tb)
                    out.append(act(E[:, o:o + n], E[:, o:o + n], ACT.Exp, tks[j], scale=-1.0, bias=sb8[:, j:j + 1],
                                   accum_out=sb8[:, 2 + j:3 + j]))
                if snk is not None:
                    out.append(tt(sb8[:, 2:3], sb8[:, 2:3], sb8[:, 8:9], ALU.add, out[0], ex))
                np_ = len(parts)
                t = recip(sb8[:, 4:4 + np_], sb8[:, 2:2 + np_], out)
                if post is not None:
                    t = tt(sb8[:, 4:4 + np_], sb8[:, 4:4 + np_], post[0](h, tb), ALU.mult, t, post[1])
                u["n"] = []
                for j, p in enumerate(parts):
                    o, n = p["off"], p["n"](tb)
                    u["n"].append(ts(E[:, o:o + n], E[:, o:o + n], sb8[:, 4 + j:5 + j], None, ALU.mult, None, t))
                smfree[i] = u["n"]

            def s3(u):
                h, tb = u["h"], u["tb"]
                if tb == 0:
                    k1, PT, f1 = PR.take()
                    heads[h] = dict(k=k1, PT=PT, fr=f1, toks=[])
                    if extra is not None:
                        k2, PC, f2 = CR.take()
                        heads[h].update(ck=k2, PC=PC, cfr=f2)
                H = heads[h]
                kb, bank, fr = bb.take()
                blocks = []
                for p in parts:
                    for b in range(p["nkb"](tb)):
                        blocks.append((p["slot"] + b, p["off"] + 128 * b))
                for i, (slot, c) in enumerate(blocks):
                    t = transpose(bank[:, 128 * slot:128 * slot + 128], u["E"][:, c:c + 128], u["n"], fr,
                                  inc=(i == len(blocks) - 1))
                ER.give(u["e"], [t])
                dst = H["PT"][:, :, 128 * tb:128 * tb + 128]
                src = bank[:, :].rearrange("p (a b) -> p a b", a=4)
                if len(blocks) == 4:
                    tc = act(dst, src, ACT.Copy, t, H["fr"])
                else:
                    step_ = blocks[1][0] - blocks[0][0] if len(blocks) > 1 else 1
                    sl = slice(blocks[0][0], blocks[-1][0] + 1, step_)
                    tc = act(dst[:, sl, :], src[:, sl, :], ACT.Copy, t, H["fr"])
                bb.give(kb, [tc])
                H["toks"].append(tc)

            def s4(u):
                h, tb = u["h"], u["tb"]
                if tb == 0:
                    return
                H = heads[h]
                kb, bank, fr = bb.take()
                ops = []
                for p in parts:
                    for b in range(p["nkb"](1)):
                        lo = 0 if b < p["nkb"](0) else 128
                        ops.append((p["v"](h, b), H["PT"][:, p["slot"] + b, lo:S], lo, p["vtok"]))
                tcp = None
                if extra is not None:
                    for z in range(2):
                        t = transpose(bank[0:15, 256 + 128 * z:384 + 128 * z], pc[:, z, h, :], extra["tok"], fr, inc=(z == 1))
                    tcp = act(H["PC"][0:15, :], bank[0:15, 256:512], ACT.Copy, t, H["cfr"])
                for i, (v, pt, lo, vt) in enumerate(ops):
                    t = mm(bank[:, lo:S], v, pt, i == 0, extra is None and i == len(ops) - 1, H["toks"], fr, vt, tcp,
                           inc=(extra is None and i == len(ops) - 1))
                if extra is not None:
                    t = mm(bank[:, 0:S], vcs[0:15, h // 4, :], H["PC"][0:15, :], False, True, tcp, extra["vtok"], inc=True)
                    CR.give(H["ck"], [t])
                PR.give(H["k"], [t])
                tk = split(op, [kt0 + h], 0, S, bank[:, 0:S].unsqueeze(1), t, used["op"])
                bb.give(kb, tk)

            units = [dict(h=h, tb=tb) for h in range(nh) for tb in range(2)]
            n = len(units)
            for i in range(n + 3):
                for d, f in ((3, s4), (2, s3), (1, s2), (0, s1)):
                    if 0 <= i - d < n:
                        f(units[i - d])
                yield
            used["end"] = [r for r in (ER.free + PR.free + CR.free)]

        op2 = operand("2", [])
        rs = stats(memx, t_x0, st[:, 0:2])
        lanes["small"].append(turn(memx, t_x0, rs, op2, gain["mem"], None, t_cols, []))
        drain("small")
        rs = stats(x, t_x, st[:, 2:4])
        op1 = operand("1", [])
        spawn("small", turn(x, t_x, rs, op1, gain["mix"], None, t_cols, []))

        k, e0, fr = eb.take()
        for g in range(4):
            t = transpose(e0[:, 128 * g:128 * g + 128], wsr[:, g, :], t_ws, fr, inc=(g == 3))
        t_wsT = tt(wsT[:, :, :], e0[:, :].rearrange("p (a b) -> p a b", a=4),
                   trl[:, :].unsqueeze(1).broadcast_to([128, 4, 128]), ALU.mult, t, t_cst)
        eb.give(k, [t_wsT])

        mods_start(0, 8, "col", 0.42)
        w_in, w_kv = a["w_in"][0], a["xattn_wkv"][0]
        t_mk, t_mv = [], []
        gemm(op2, w_kv, 0, 0, 512, range(16), to_heads(mk_t, 0, used=[], done=t_mk))
        gemm(op2, w_kv, 0, 512, 512, range(16), to_rows(mv_t, 0, 512, 0, ACT.Copy, [], t_mv))
        drain("small")
        tq, tk_, tv_ = [], [], []
        gemm(op1, w_in, 0, 1024, 512, range(16), to_heads(bq, 0, done=tq))
        gemm(op1, w_in, 0, 1536, 512, range(16), to_heads(bk, 0, done=tk_))
        gemm(op1, w_in, 0, 2048, 512, range(16), to_rows(bv, 0, 512, 0, ACT.Copy, [], tv_))
        drain("small")

        t_sv = []

        def epi_v(p, t, release):
            def run():
                while not stgs.ready():
                    yield
                k, sg, fr = stgs.take()
                t0 = [act(sg[:, tb, :], p[tb][:, :], ACT.Gelu_apprx_tanh, t, fr,
                          accum_out=ln4[:, tb:tb + 1]) for tb in range(2)]
                release(t0)
                yield
                tn = []
                for tb in range(2):
                    m, v = ln4[:, tb:tb + 1], ln4[:, 2 + tb:3 + tb]
                    t1 = ts(m, m, 1.0 / 512, None, ALU.mult, None, t0[tb])
                    t2 = ts(sg[:, tb, :], sg[:, tb, :], m, None, ALU.subtract, None, t1)
                    t3 = act(sv[:, tb, :], sg[:, tb, :], ACT.Square, t2, accum_out=v)
                    t4 = rstd_of(v, 512, v, t3)
                    t5 = DV(lambda e, tb=tb, v=v: e.scalar_tensor_tensor(
                        out=sg[:, tb, :], in0=sg[:, tb, :], scalar=v, in1=lng[:, :], op0=ALU.mult, op1=ALU.mult),
                        t4, t_ln)
                    tn.append(tt(sg[:, tb, :], sg[:, tb, :], lnb[:, :], ALU.add, t5))
                    yield
                for tb in range(2):
                    while not eb.ready():
                        yield
                    kb, e, fb = eb.take()
                    for g in range(4):
                        t6 = mm(e[:, 128 * g:128 * g + 128], wsT[:, g, :], sg[:, tb, 128 * g:128 * g + 128],
                                True, True, tn[tb], fb, t_wsT, inc=(g == 3))
                    t7 = tt(sv[:, tb, :].rearrange("p (a b) -> p a b", a=4), e[:, :].rearrange("p (a b) -> p a b", a=4),
                            bc(bsT, 128), ALU.add, t6, t_cols2)
                    eb.give(kb, [t7])
                    t_sv.append(t7)
                    yield
                stgs.give(k, [t6])
            spawn("small", run())

        op2m = operand("2", [])

        def epi_u(p, t, release):
            def run():
                while not stgs.ready():
                    yield
                k, sg, fr = stgs.take()
                t0 = [act(sg[:, tb, :], p[tb][:, :], ACT.Gelu_apprx_tanh, t, fr) for tb in range(2)]
                release(t0)
                t1 = tt(sg[:, :, :], sg[:, :, :], sv[:, :, :], ALU.mult, t0, t_sv)
                yield
                for i in range(0, 4, 2):
                    while not eb.ready():
                        yield
                    kb, e, fb = eb.take()
                    for h in range(2):
                        for tb in range(2):
                            t2 = transpose(e[:, 256 * h + 128 * tb:256 * h + 128 * tb + 128],
                                           sg[:, tb, 128 * (i + h):128 * (i + h) + 128], t1, fb, inc=(h == 1 and tb == 1))
                    eb.give(kb, split(op2m, [i, i + 1], 0, S, e[:, :].rearrange("p (a b) -> p a b", a=2), t2, op2.read))
                    yield
                stgs.give(k, [t2])
            spawn("small", run())


        use = {"scr": [XN["free"], XN["yb"]], "op": op2.read}
        tri = lambda tb: (lmk[:, 128:256] if tb == 0 else lmk[:, 0:256])
        spawn("big", attention(
            4, lambda h, tb: bq[:, h, 128 * tb:128 * tb + 128],
            [dict(k=lambda h, tb: [(bk[:, h, 0:128 * tb + 128], 0)], off=0, n=lambda tb: 128 * tb + 128, mask=tri,
                  slot=0, v=lambda h, b: bv[:, b, 128 * h:128 * h + 128], nkb=lambda tb: tb + 1,
                  tok=[tk_, t_cst], vtok=tv_)], op2m, 4, use, tq))

        gemm(op1, w_in, 0, 512, 512, range(16), epi_v)
        gemm(op1, w_in, 0, 0, 512, range(16), epi_u)
        t_cc, t_cq, t_ck, t_cv = [], [], [[], []], [[], []]
        drain("big")
        gemm(op1, w_in, 0, 3584, 512, range(16), to_heads(cc, 0, done=t_cc))
        drain("small")

        t_cb = []
        for m in range(2):
            for g in range(2):
                src = cc[:, 2 * m + g, :]
                for half in range(2):
                    i0 = src[:, 16 * half:16 * half + 240].rearrange("p (n l) -> p l n", l=16)
                    t_cb.append(tt(cb[:, m, 16 * half:16 * half + 16, 15 * g:15 * g + 15], i0,
                                   bc(posT[:, 16 * half:16 * half + 16], 15), ALU.add, t_cc, t_cols2, use["end"]))
        t_h = []

        def compress():
            for m, w1 in ((0, a["cmp_k_w1"][0]), (1, a["cmp_v_w1"][0])):
                k, e, fr = bb.take()
                for c in range(4):
                    src = w1[1024 * c:1024 * c + 1024, :].rearrange("(l d) o -> d l o", d=128)
                    j, (landed, _, _, _) = chunk("r", src, (8, 128))
                    rv = view(raws[j % NRAW], (8, 128))
                    for l in range(8):
                        t = mm(e[:, 0:30], rv[:, l, :], cb[:, m, 8 * c + l, :], c == 0 and l == 0, c == 3 and l == 7,
                               landed, t_cb, fr, inc=(l == 7))
                    raw_free[j] = t
                    yield
                t1 = act(hT[:, m, 0:30], e[:, 0:30], ACT.Gelu_apprx_tanh, t)
                t_h.append(t1)
                bb.give(k, [t1])
                yield
            k, e, fr = bb.take()
            mm(e[:, 0:30], wk2[:, 0, :], hT[:, 0, 0:30], True, True, t_h, t_w2, fr)
            for g in range(2):
                t = mm(e[0:15, 128 + 128 * g:256 + 128 * g], hT[:, 1, 15 * g:15 * g + 15], wk2[:, 1, :], True, True,
                       inc=(g == 1))
            t1 = copy(kcT[:, 0:30], e[:, 0:30], t)
            t2 = copy(vcs[0:15, :, :], e[0:15, 128:384].rearrange("p (a b) -> p a b", a=2), t)
            bb.give(k, [t1, t2])
            t_h.extend([t1, t2])

        spawn("big", compress())
        gemm(op1, w_in, 0, 2560, 512, range(16), to_heads(cq, 0, done=t_cq))
        gemm(op1, w_in, 0, 3072, 512, range(16), to_heads(cq, 4, done=t_cq))
        for i in range(2):
            gemm(op1, w_in, 0, 4096 + 512 * i, 512, range(16),
                 two(to_heads(ckT[i], 0, done=t_ck[i], nh=2), to_rows(cv[i], 0, 256, 256, ACT.Copy, [], t_cv[i])))
        t_cg = []
        gemm(op1, w_in, 0, 5120, 24, range(16), to_rows(cg, 0, 24, 0, ACT.Sigmoid, [], t_cg))
        drain("big")
        drain("small")
        t_op1 = op1.read

        t_pc = []
        for tb in range(2):
            k, e, fr = bb.take()
            for h in range(8):
                t = mm(e[:, 15 * h:15 * h + 15], cq[:, h, 128 * tb:128 * tb + 128], kcT[:, 15 * (h // 4):15 * (h // 4) + 15],
                       True, True, t_cq, t_h, fr, inc=(h == 7))
            P = pc[:, tb, :, :]
            m8 = sm[:, 8 * tb:8 * tb + 8]
            d8 = sm[:, 16 + 8 * tb:24 + 8 * tb]
            t1 = tt(P, e[:, 0:120].rearrange("p (a b) -> p a b", a=8),
                    cmk[:, 15 * tb:15 * tb + 15].unsqueeze(1).broadcast_to([128, 8, 15]), ALU.add, t, t_cst)
            bb.give(k, [t1])
            t2 = DV(lambda e, P=P, m8=m8: e.tensor_reduce(m8, P, AX, ALU.max), t1, use["end"])
            t3 = tt(P, P, bc(m8, 15), ALU.subtract, t2)
            t4 = act(P, P, ACT.Exp, t3, scale=SC)
            t5 = DV(lambda e, P=P, d8=d8: e.tensor_reduce(d8, P, AX, ALU.add), t4)
            t6 = recip(d8, d8, t5)
            gv = cg[:, tb, :].rearrange("p (h j) -> p h j", j=3)
            t7 = DV(lambda e, d8=d8, gv=gv, tb=tb: e.scalar_tensor_tensor(
                out=d8, in0=d8, scalar=cmk[:, 30 + tb:31 + tb], in1=gv[:, :, 0], op0=ALU.mult, op1=ALU.mult), t6, t_cg)
            t_pc.append(tt(P, P, bc(d8, 15), ALU.mult, t7))

        cmask = lambda tb: (mskt[:, 512:640] if tb == 0 else mskt[:, 384:640])
        use2 = {"scr": [use["end"], t_h, t_pc], "op": op2.read}
        cparts = [dict(k=lambda h, tb, i=i: [(ckT[i][:, h // 4, 0:128 * tb + 128], 256 * i)], off=256 * i,
                       n=lambda tb: 128 * tb + 128, mask=cmask, slot=2 * i,
                       v=lambda h, b, i=i: cv[i][:, b, 128 * (h // 4):128 * (h // 4) + 128],
                       nkb=lambda tb: tb + 1, tok=[t_ck[i], t_c], vtok=t_cv[i]) for i in range(2)]
        spawn("big", attention(
            8, lambda h, tb: cq[:, h, 128 * tb:128 * tb + 128], cparts, op2m, 8, use2, t_cq,
            post=(lambda h, tb: cg[:, tb, 3 * h + 1:3 * h + 3], t_cg), extra={"tok": t_pc, "vtok": t_h}))
        w_out = a["w_out"][0]
        for n in range(4):
            gemm(op2m, w_out, 0, 512 * n, 512, range(8), residual(n, False))
        drain("big")
        XN["free"] = [use2["end"]]
        XN["yb"] = [[use2["end"]], [use2["end"]]]
        for n in range(4):
            gemm(op2m, w_out, 1024, 512 * n, 512, range(8, 16), residual(n, True))

        def norm_turn(nm, used, g, sh=None, gtok=None, wait=0):
            rs = sums(st[:, 4:6], RES["ss"])
            RES["ss"] = []
            op = operand(nm, used)
            lanes["small"].insert(0, turn(x, RES["tok"], rs, op, g, sh, gtok or t_cols, used))
            while lanes["small"]:
                step("small")
            for i in range(8):
                RES["tok"][i] = RES["tok"][i] + XN["free"]
            return op

        opx = norm_turn("1", t_op1, gain["xa"])
        xq_t = []
        gemm(opx, a["xattn_wq"][0], 0, 0, 512, range(16), to_heads(bq, 0, used=[use2["end"]], done=xq_t))
        drain("small")
        zero = lambda tb: mskt[:, 128:384]
        use3 = {"scr": [XN["free"], XN["yb"]], "op": op2m.read}
        opo = operand("2", [])
        spawn("big", attention(
            4, lambda h, tb: bq[:, h, 128 * tb:128 * tb + 128],
            [dict(k=lambda h, tb: [(mk[:, h, :], 0)], off=0, n=lambda tb: 256, mask=zero, slot=0,
                  v=lambda h, b: mv[:, b, 128 * h:128 * h + 128], nkb=lambda tb: 2, tok=[t_mk, t_c], vtok=t_mv)],
            opo, 0, use3, xq_t))
        drain("big")
        XN["free"] = [use3["end"]]
        XN["yb"] = [[use3["end"]], [use3["end"]]]
        for n in range(4):
            gemm(opo, a["xattn_wo"][0], 0, 512 * n, 512, range(4), residual(n, True))

        opm = norm_turn("1", opx.read, gain["mlp"])

        def hidden(op, kt, used, fn):
            def epi(p, t, release):
                def run():
                    while not stgs.ready():
                        yield
                    k, sg, fr = stgs.take()
                    t1 = fn(p, t, sg, fr, release)
                    yield
                    for i in range(0, 4, 2):
                        while not eb.ready():
                            yield
                        kb, e, fb = eb.take()
                        for h in range(2):
                            for tb in range(2):
                                t2 = transpose(e[:, 256 * h + 128 * tb:256 * h + 128 * tb + 128],
                                               sg[:, tb, 128 * (i + h):128 * (i + h) + 128], t1, fb,
                                               inc=(h == 1 and tb == 1))
                        eb.give(kb, split(op, [kt + i, kt + i + 1], 0, S,
                                          e[:, :].rearrange("p (a b) -> p a b", a=2), t2, used))
                        yield
                    stgs.give(k, [t2])
                spawn("small", run())
            return epi

        def relu2(p, t, sg, fr, release):
            t0 = [act(sg[:, tb, :], p[tb][:, :], ACT.Relu, t, fr) for tb in range(2)]
            release(t0)
            return PO(lambda e: e.tensor_tensor(sg[:, :, :], sg[:, :, :], sg[:, :, :], ALU.mult), t0)

        w_up, w_down = a["w_up"][0], a["w_down"][0]
        used_h = {"2": list(flat([opo.read])), "3": [use3["end"], t_pc, use2["end"]]}

        def up(s):
            nm = "23"[s % 2]
            op = operand(nm, [])
            for i in range(4):
                gemm(opm, w_up, 0, 2048 * s + 512 * i, 512, range(16), hidden(op, 4 * i, used_h[nm], relu2))
            return op

        def down(s, op):
            for n in range(4):
                gemm(op, w_down, 2048 * s, 512 * n, 512, range(16), residual(n, s == 3))
            used_h["23"[s % 2]] = op.read

        mods_start(12, 20, "col", 0.3)
        ho = up(0)
        for s in range(1, 4):
            drain("small")
            nx = up(s)
            drain("small")
            down(s - 1, ho)
            ho = nx
        drain("small")
        mods_finish()
        t_g2 = []
        g_x = gmod[:, 0, :]
        t_a = ts(g_x, modx[:, 16:32], 1.0, None, ALU.add, None, MD["xdone"])
        t_g2.append(tt(g_x, g_x, gain["mix2"], ALU.mult, t_a, t_cols))
        ctxx = sb_ctx
        t_ctx = load(ctxx[:, :, :], a["ctx_2"][0].rearrange("(t p) d -> p t d", p=128), opm.read, q=PO)
        rs = stats(ctxx, t_ctx, st[:, 6:8])
        opc = operand("2", [])
        spawn("small", turn(ctxx, t_ctx, rs, opc, g_x, modx[:, 0:16], [t_g2, MD["xdone"]], used_h["2"]))
        down(3, ho)
        drain("small")
        ctx_used = list(flat([XN["free"]]))

        t_fn = load(gt[:, :], a["final_norm"].rearrange("(a n) -> a n", a=1).broadcast_to([128, D]), use3["end"], t_mk, t_mv,
                    opo.tok, q=PO)
        rs = sums(st[:, 8:10], RES["ss"])
        RES["ss"] = []
        for tb in range(2):
            t1 = DV(lambda e, tb=tb: e.scalar_tensor_tensor(out=x[:, tb, :], in0=x[:, tb, :], scalar=st[:, 8 + tb:9 + tb],
                                                           in1=gt[:, :], op0=ALU.mult, op1=ALU.mult),
                    rs[tb][1], t_fn, RES["tok"])
            for n in range(4):
                RES["tok"][2 * n + tb] = [t1]
        t_gt0 = list(RES["tok"][0] + RES["tok"][1])
        t_cst2 = [load(ropc[:, :, :], cd[:, ROC:ROC + 256].rearrange("p (a b) -> p a b", a=2), t_sv, t_ln, use["end"], op2m.tok, q=PO),
                  load(rops[:, :, :], cd[:, ROS:ROS + 256].rearrange("p (a b) -> p a b", a=2), q=PO),
                  load(chm[:, :], cd[:, HGM + 768:HGM + 772], q=PO),
                  load(hgm[:, :, :], cd[:, HGM:HGM + 768].rearrange("p (a b) -> p a b", a=6), q=PO)]

        def gates_start(j0, used, rate):
            mods_finish()
            MD["gtb"] = load(gt[:, :], b_mod[:, 512 * j0:512 * j0 + 2048].broadcast_to([128, D]), used, q=PO)
            MD["gt"] = []
            mods_start(j0, j0 + 4, "row", rate)

        g_l = gmod[:, 1, :]
        t_a = ts(g_l, mod[:, 16:32], 1.0, None, ALU.add, None, MD["done"])
        t_gl = tt(g_l, g_l, gain["mix2"], ALU.mult, t_a, t_cols)
        rs = stats(x, RES["tok"], st[:, 10:12])
        op1 = operand("1", [])
        spawn("small", turn(x, RES["tok"], rs, op1, g_l, mod[:, 0:16], [t_gl, MD["done"]], [opm.read, ctx_used]))
        gates_start(8, t_gt0, 0.3)

        w2 = a["w_in_2"][0]
        G = {"free": [list(ctx_used), ho.read], "lbfree": ho.read, "hv": [], "hq": []}
        tS0 = []

        def bounds(g, d, used):
            c0 = 512 * g
            t1 = load(lb[:, 0, :], a["hg_lb_2"][0, d:d + 1, c0:c0 + 512].broadcast_to([128, 512]), used, q=PO)
            t2 = load(lb[:, 1, :], a["hg_lb_2"][1, d:d + 1, c0:c0 + 512].broadcast_to([128, 512]), used, q=PO)
            t3 = tt(lb[:, 0, :], lb[:, 0, :], lb[:, 1, :], ALU.subtract, t1, t2)
            t4 = act(lb[:, 1, :], lb[:, 0, :], ACT.Sigmoid, t3, scale=-1.0)
            return [t4, act(lb[:, 0, :], lb[:, 0, :], ACT.Sigmoid, t4)]

        def forget(p, t, release, g, d, latl):
            tb_ = bounds(g, d, G["lbfree"])
            fr = G["free"]
            t0 = [act(hA[:, tb, :], p[tb][:, :], ACT.Sigmoid, t, fr) for tb in range(2)]
            release(t0)
            t1 = tt(hA[:, :, :], hA[:, :, :], lb[:, 1, :].unsqueeze(1).broadcast_to([128, 2, 512]), ALU.mult, t0, tb_)
            t2 = tt(hA[:, :, :], hA[:, :, :], lb[:, 0, :].unsqueeze(1).broadcast_to([128, 2, 512]), ALU.add, t1)
            G["lbfree"] = [t2]
            t3 = ts(hK[:, :, :], hA[:, :, :], -1.0, 1.0, ALU.mult, ALU.add, t2, fr)
            t4 = act(hA[:, :, :], hA[:, :, :], ACT.Ln, t2, t3)
            yield
            e3 = []
            for tb in range(2):
                k, e, fb = bb.take()
                if latl:
                    t5 = mm(e[:, :], hgm[:, 2 + d, :], hA[:, tb, :], True, True, t4, fb, t_cst2, inc=True)
                else:
                    far = tb == (0 if d == 0 else 1)
                    t5 = mm(e[:, :], hgm[:, 4 + d, :], hA[:, tb, :], True, not far, t4, fb, t_cst2, inc=not far)
                    if far:
                        t5 = mm(e[:, :], ones[:, :], hA[:, 1 - tb, :], False, True, inc=True)
                t6 = act(hE[:, tb, :], e[:, :], ACT.Exp, t5, fr)
                bb.give(k, [t6])
                e3.append(t6)
            t7 = tt(hE[:, :, :], hE[:, :, :], hK[:, :, :], ALU.mult, e3, t3)
            yield
            return t3, t4, t7

        def ctx_gate(g, d):
            def epi(p, t, release):
                def run():
                    t3, t4, t7 = yield from forget(p, t, release, g, d, False)
                    k, e, fb = bb.take()
                    for h in range(4):
                        for tb in range(2):
                            t8 = mm(e[:, 128 * h:128 * h + 128], hE[:, tb, 128 * h:128 * h + 128],
                                    hV[:, tb, 128 * h:128 * h + 128], tb == 0, tb == 1, t7, fb, G["hv"],
                                    inc=(h == 3 and tb == 1))
                    t9 = act(S0[:, 8 * d + 4 * g:8 * d + 4 * g + 4, :], e[:, :].rearrange("p (a b) -> p a b", a=4),
                             ACT.Copy, t8, ctx_used)
                    bb.give(k, [t9])
                    tS0.append(t9)
                    G["free"] = [t8, t9]
                    yield
                spawn("big", run())
            return epi

        for g in range(2):
            hv = []
            drain("big")
            gemm(opc, w2, 0, 3072 + 512 * g, 512, range(16), to_rows(hV, 0, 512, 0, ACT.Copy, G["free"], hv))
            G["hv"] = hv
            for d in range(2):
                gemm(opc, w2, 0, 1024 + 1024 * d + 512 * g, 512, range(16), ctx_gate(g, d))
        drain("big")

        t_qkg = []

        def qk_epi(nh, gi, dst, h0, rot, used, done):
            def epi(p, t, release):
                def run():
                    w = 128 * nh
                    while not stgs.ready():
                        yield
                    k, sg, fr = stgs.take()
                    rr = RT["free"]
                    ss = sm[:, 0:2 * nh].rearrange("p (a b) -> p a b", a=2)
                    t0 = [act(sg[:, tb, 0:w], p[tb][:, 0:w], ACT.Copy, t, fr) for tb in range(2)]
                    t1 = [act(rt[:, tb, 0:w], p[tb][:, 0:w], ACT.Square, t, rr) for tb in range(2)]
                    release(t0 + t1)
                    yield
                    v4 = lambda z, tb: z[:, tb, 0:w].rearrange("p (h d) -> p h d", h=nh)
                    t2 = [DV(lambda e, tb=tb: e.tensor_reduce(ss[:, tb, :], v4(rt, tb), AX, ALU.add), t1, rr)
                          for tb in range(2)]
                    s2 = sm[:, 0:2 * nh]
                    t3 = rstd_of(s2, 128, s2, t2)
                    t4 = [tt(v4(sg, tb), v4(sg, tb), bc(ss[:, tb, :], 128), ALU.mult, t3, t0) for tb in range(2)]
                    t5 = [tt(v4(sg, tb), v4(sg, tb), qkg[:, gi, :].unsqueeze(1).broadcast_to([128, nh, 128]),
                             ALU.mult, t4, t_qkg) for tb in range(2)]
                    yield
                    tl = t5
                    if rot:
                        t6 = []
                        for tb in range(2):
                            t6.append(tt(v4(rt, tb), v4(sg, tb), ropc[:, tb, :].unsqueeze(1).broadcast_to([128, nh, 128]),
                                         ALU.mult, t5, t_cst2, t2))
                            sv_ = sg[:, tb, 0:w].rearrange("p (h z f) -> p h z f", z=4, f=32)
                            dv_ = rt2[:, tb, 0:w].rearrange("p (h z f) -> p h z f", z=4, f=32)
                            rs_ = rops[:, tb, :].rearrange("p (z f) -> p z f", z=4)
                            for zz in range(4):
                                t6.append(tt(dv_[:, :, zz, :], sv_[:, :, zz ^ 1, :],
                                             rs_[:, zz, :].unsqueeze(1).broadcast_to([128, nh, 32]), ALU.mult, t5, rr))
                        tl = [tt(sg[:, :, 0:w], rt[:, :, 0:w], rt2[:, :, 0:w], ALU.add, t6)]
                        yield
                    RT["free"] = [tl]
                    for i in range(0, nh, 2):
                        while not eb.ready():
                            yield
                        kb, e, fb = eb.take()
                        for h in range(2):
                            for tb in range(2):
                                t7 = transpose(e[:, 256 * h + 128 * tb:256 * h + 128 * tb + 128],
                                               sg[:, tb, 128 * (i + h):128 * (i + h) + 128], tl, fb,
                                               inc=(h == 1 and tb == 1))
                        t8 = act(dst[:, h0 + i:h0 + i + 2, :], e[:, :].rearrange("p (a b) -> p a b", a=2), ACT.Copy, t7, used)
                        eb.give(kb, [t8])
                        done.append(t8)
                        yield
                    stgs.give(k, [t7])
                spawn("small", run())
            return epi

        RT = {"free": list(flat([G["free"], G["lbfree"]]))}

        def load_qkg(used):
            t_qkg.clear()
            t_qkg.extend([load(qkg[:, 0, :], a["q_norm_g_2"].broadcast_to([128, 128]), used, q=PO),
                          load(qkg[:, 1, :], a["k_norm_g_2"].broadcast_to([128, 128]), used, q=PO)])

        load_qkg(RT["free"])
        t_xk, t_xv = [], []
        gemm(opc, w2, 0, 6144, 512, range(16),
             two(qk_epi(2, 1, xkT, 0, False, ctx_used, t_xk), to_rows(xv, 0, 256, 256, ACT.Copy, ctx_used, t_xv)))
        drain("small")
        op2m = operand("2", [])
        mix_used = opc.read
        G["free"] = [G["free"], RT["free"]]
        G["lbfree"] = [G["lbfree"], RT["free"]]
        G["qo"] = [RT["free"]]

        E1R, E2R, STR, HSR = Ring(hE1), Ring(hE2), Ring(hST), Ring(hS)
        HMR = Ring(hM)
        HQ = {"tok": [], "free": [], "o": [], "ofree": []}

        def lat_gate(g, d):
            def epi(p, t, release):
                def run():
                    t3, t4, t7 = yield from forget(p, t, release, g, d, True)
                    last = []
                    for h in range(4):
                        hs = slice(128 * h, 128 * h + 128)
                        k, e, fb = bb.take()
                        for tb in range(2):
                            mm(e[:, 128 * tb:128 * tb + 128], hA[:, tb, hs], hgm[:, d, :], True, True, t4, fb, t_cst2)
                        for tb in range(2):
                            t5 = transpose(e[:, 256 + 128 * tb:384 + 128 * tb], hK[:, tb, hs], t3, inc=(tb == 1))
                        k1, E1, f1 = E1R.take()
                        k2, E2, f2 = E2R.take()
                        t6 = act(E1[:, :], e[:, 0:256], ACT.Exp, t5, f1, G["e"])
                        t8 = act(E2[:, :], e[:, 0:256], ACT.Exp, t5, f2, G["e"], scale=-1.0)
                        dsl = E1[:, :].rearrange("p (c t) -> p c t", t=32)[:, :, 31 if d == 0 else 0]
                        dd = dec[:, h % 2, :]
                        t9 = copy(dd, dsl, t6, G["dec"][h % 2])
                        t10 = tt(E2[:, :], e[:, 256:512], E2[:, :], ALU.mult, t8)
                        bb.give(k, [t6, t8, t10])
                        t11 = tt(E1[:, :], E1[:, :], hQ[:, h, :], ALU.mult, t9, t6, HQ["tok"])
                        yield
                        k, e, fb = bb.take()
                        for tb in range(2):
                            t12 = mm(e[:, 128 * tb:128 * tb + 128], E2[:, 128 * tb:128 * tb + 128],
                                     E1[:, 128 * tb:128 * tb + 128], True, True, t10, t11, fb, inc=(tb == 1))
                        E2R.give(k2, [t12])
                        ks, ST, fs = STR.take()
                        t13 = tt(ST[:, :, :], e[:, 0:256].rearrange("p (a b) -> p a b", a=2),
                                 hgm[:, d, :].unsqueeze(1).broadcast_to([128, 2, 128]), ALU.mult, t12, fs, G["e"])
                        bb.give(k, [t13])
                        kh, HS, fh = HSR.take()
                        seq = list(range(8)) if d == 0 else list(range(7, -1, -1))
                        tc = copy(HS[:, seq[0], :], S0[:, 8 * d + 4 * g + h, :], fh, tS0, G["e"])
                        kk, eU, fU = bb.take()
                        kk2, eU2, fU2 = bb.take()
                        tus = {}
                        for tb, bank, w in ((0, eU, fU), (1, eU2, fU2)):
                            km, VM, fm = HMR.take()
                            tm = PO(lambda e_, VM=VM, tb=tb, hs=hs: e_.tensor_tensor(
                                VM[:, :, :], hV[:, tb, hs].unsqueeze(1).broadcast_to([128, 4, 128]),
                                bc(chm[:, :], 128), ALU.mult), G["hv"], fm, G["e"], t_cst2)
                            tus[tb] = mm(bank[:, :], hE[:, tb, hs], VM[:, :, :], True, True, t7, w, tm, inc=True)
                            HMR.give(km, [tus[tb]])
                        for c in seq[:7]:
                            tb = c // 4
                            bank, tu = (eU, eU2)[tb], tus[tb]
                            col = 128 * (c % 4)
                            nx = seq[seq.index(c) + 1]
                            tc = DV(lambda e_, c=c, nx=nx, bank=bank, col=col, dd=dd, HS=HS: e_.scalar_tensor_tensor(
                                out=HS[:, nx, :], in0=HS[:, c, :], scalar=dd[:, c:c + 1], in1=bank[:, col:col + 128],
                                op0=ALU.mult, op1=ALU.add), tu, tc, t9)
                        G["dec"][h % 2] = tc
                        bb.give(kk, [tc])
                        bb.give(kk2, [tc])
                        yield
                        k, e, fb = bb.take()
                        for tb in range(2):
                            mm(e[:, 128 * tb:128 * tb + 128], hV[:, tb, hs], ST[:, tb, :], tb == 0, False, t13, fb, G["hv"])
                        for i, c in enumerate(range(8)):
                            t14 = mm(e[:, 32 * c:32 * c + 32], HS[:, c, :], E1[:, 32 * c:32 * c + 32], False, i == 7, tc,
                                     inc=(i == 7))
                        STR.give(ks, [t14])
                        HSR.give(kh, [t14])
                        E1R.give(k1, [t14])
                        if d == 0:
                            t15 = act(hO[:, h, :], e[:, 0:256], ACT.Copy, t14, HQ["ofree"])
                            HQ["o"].append(t15)
                        else:
                            t15 = tt(hO[:, h, :], e[:, 0:256], hO[:, h, :], ALU.add, t14, HQ["o"])
                            HQ["o2"].append(t15)
                        bb.give(k, [t15])
                        last = [t14, t15]
                        yield
                    G["free"] = [t14, t15]
                spawn("big", run())
            return epi

        def readout(g):
            def epi(p, t, release):
                def run():
                    while not stgs.ready():
                        yield
                    ks, sg, fr = stgs.take()
                    t0 = [act(sg[:, tb, :], p[tb][:, :], ACT.Silu, t, fr) for tb in range(2)]
                    release(t0)
                    yield
                    for i in range(2):
                        hh = slice(2 * i, 2 * i + 2)
                        A = hA[:, i, :]
                        A3 = A.rearrange("p (a b) -> p a b", a=2)
                        t1 = act(A3, hO[:, hh, :], ACT.Square, HQ["o2"], G["free"])
                        k, e, fb = bb.take()
                        t2 = mm(e[:, :], ones[:, :], A, True, True, t1, fb, inc=True)
                        t3 = ts(A, e[:, :], 1.0 / 128, EPS, ALU.mult, ALU.add, t2)
                        bb.give(k, [t3])
                        t4 = act(A, A, ACT.Sqrt, t3)
                        t5 = recip(A, A, t4)
                        t6 = DV(lambda e, A3=A3, hh=hh: e.scalar_tensor_tensor(
                            out=A3, in0=hO[:, hh, :], scalar=hgn, in1=A3, op0=ALU.mult, op1=ALU.mult), t5, t_cols2)
                        yield
                        kb, e, fb = bb.take()
                        for h in range(2):
                            for tb in range(2):
                                t7 = transpose(e[:, 256 * h + 128 * tb:256 * h + 128 * tb + 128],
                                               sg[:, tb, 128 * (2 * i + h):128 * (2 * i + h) + 128], t0, fb,
                                               inc=(h == 1 and tb == 1))
                        t8 = tt(A, A, e[:, :], ALU.mult, t6, t7)
                        bb.give(kb, [t8])
                        kt = 4 * g + 2 * i
                        tk = split(op2m, [kt, kt + 1], 0, S, A3, t8, mix_used)
                        G["free"] = [G["free"], tk]
                        HQ["ofree"] = [HQ["ofree"], t6]
                        yield
                    stgs.give(ks, [t7])
                spawn("big", run())
            return epi

        G["e"] = [list(flat([G["free"]]))]
        G["dec"] = [None, None]
        HQ["ofree"] = [RT["free"]]
        for g in range(2):
            HQ["o"], HQ["o2"], hv, hq = [], [], [], []
            drain("small")
            gemm(op1, w2, 0, 3072 + 512 * g, 512, range(16), to_rows(hV, 0, 512, 0, ACT.Copy, [G["free"]], hv))
            gemm(op1, w2, 0, 512 * g, 512, range(16), to_heads(hQ, 0, ACT.Silu, used=[G["free"], RT["free"]], done=hq))
            drain("small")
            G["hv"], HQ["tok"] = hv, hq
            for d in range(2):
                gemm(op1, w2, 0, 1024 + 1024 * d + 512 * g, 512, range(16), lat_gate(g, d))
            gemm(op1, w2, 0, 4096 + 512 * g, 512, range(16), readout(g))
            drain("big")

        end = [G["free"], G["lbfree"], HQ["ofree"]]
        RT["free"] = list(flat(end))
        load_qkg(end)
        t_lk, t_lv, t_lq = [], [], []
        gemm(op1, w2, 0, 6144, 512, range(16),
             two(qk_epi(2, 1, lkT, 0, True, end, t_lk), to_rows(lv, 0, 256, 256, ACT.Copy, end, t_lv)))
        drain("small")
        gemm(op1, w2, 0, 5120, 512, range(16), qk_epi(4, 0, lq, 0, True, end, t_lq))
        drain("small")
        gemm(op1, w2, 0, 5632, 512, range(16), qk_epi(4, 0, lq, 4, True, end, t_lq))
        drain("small")
        nsk = sm2[:, 0:8]
        t_nsk = ts(nsk, sink[:, :], -1.0, None, ALU.mult, None, t_sink)
        use4 = {"scr": [end], "op": mix_used}
        keys = lambda h, tb: [(lkT[:, h // 4, :], 0), (xkT[:, h // 4, :], 256)]
        vals = lambda h, b: (lv if b < 2 else xv)[:, b % 2, 128 * (h // 4):128 * (h // 4) + 128]
        spawn("big", attention(
            8, lambda h, tb: lq[:, h, 128 * tb:128 * tb + 128],
            [dict(k=keys, off=0, n=lambda tb: 512, mask=lambda tb: (mskt[:, 384:896] if tb == 0 else mskt[:, 0:512]),
                  slot=0, v=vals, nkb=lambda tb: 4, tok=[t_lk, t_xk, t_c], vtok=[t_lv, t_xv])],
            op2m, 8, use4, t_lq, snk=(sink, nsk, [t_nsk, t_sink])))
        mods_finish()
        wo2 = a["w_out_2"][0]
        for n in range(4):
            gemm(op2m, wo2, 0, 512 * n, 512, range(8), residual(n, False, scale=gt))
        drain("big")
        XN["free"] = [use4["end"]]
        XN["yb"] = [[use4["end"]], [use4["end"]]]
        for n in range(4):
            gemm(op2m, wo2, 1024, 512 * n, 512, range(8, 16), residual(n, True, scale=gt))

        t_gtu = [list(t) for t in RES["tok"]]
        t_a = ts(gmod[:, 0, :], mod[:, 48:64], 1.0, None, ALU.add, None, MD["done"], opc.tok)
        t_gf = tt(gmod[:, 0, :], gmod[:, 0, :], gain["ffn2"], ALU.mult, t_a, t_cols)
        opf = norm_turn("1", op1.read, gmod[:, 0, :], mod[:, 32:48], [t_gf, MD["done"]])
        gates_start(20, t_gtu, 0.4)
        wgu, wd2 = a["w_gate_up_2"][0], a["w_down_2"][0]
        used_h = {"2": list(flat([op2m.read])), "3": [use4["end"]] + op2m.read}

        def gate_up(s, cnt):
            nm = "23"[s % 2]
            op = operand(nm, [])
            for i in range(cnt):
                cell = {}

                def epi_g(p, t, release, cell=cell):
                    def run():
                        while not stgs.ready():
                            yield
                        cell["k"], sg, fr = stgs.take()
                        cell["sg"] = sg
                        cell["t"] = [act(sg[:, tb, :], p[tb][:, :], ACT.Silu, t, fr) for tb in range(2)]
                        release(cell["t"])
                    spawn("small", run())

                def epi_p(p, t, release, cell=cell, i=i):
                    def run():
                        sg = cell["sg"]
                        t1 = [tt(sg[:, tb, :], p[tb][:, :], sg[:, tb, :], ALU.mult, t, cell["t"]) for tb in range(2)]
                        release(t1)
                        yield
                        for q in range(0, 4, 2):
                            while not eb.ready():
                                yield
                            kb, e, fb = eb.take()
                            for h in range(2):
                                for tb in range(2):
                                    t2 = transpose(e[:, 256 * h + 128 * tb:256 * h + 128 * tb + 128],
                                                   sg[:, tb, 128 * (q + h):128 * (q + h) + 128], t1, fb,
                                                   inc=(h == 1 and tb == 1))
                            eb.give(kb, split(op, [4 * i + q, 4 * i + q + 1], 0, S,
                                              e[:, :].rearrange("p (a b) -> p a b", a=2), t2, used_h[nm]))
                            yield
                        stgs.give(cell["k"], [t2])
                    spawn("small", run())
                gemm(opf, wgu, 0, 2048 * s + 512 * i, 512, range(16), epi_g)
                gemm(opf, wgu, 0, FF2 + 2048 * s + 512 * i, 512, range(16), epi_p)
            return op

        def down2(s, op, cnt, out=None):
            for n in range(4):
                gemm(op, wd2, 2048 * s, 512 * n, 512, range(4 * cnt), residual(n, False, scale=gt, out=out))
            used_h["23"[s % 2]] = op.read

        cnts = [4, 4, 3]
        ho = gate_up(0, 4)
        for s in range(1, 3):
            drain("small")
            nx = gate_up(s, cnts[s])
            drain("small")
            mods_finish()
            down2(s - 1, ho, cnts[s - 1])
            ho = nx
        drain("small")
        down2(2, ho, 3, out=a["out"])
        return rec, dict(PE=PE, AC=AC, DV=DV, PO=PO, SP=SP)

    bmc = small("bmc", [96])
    sm2 = small("sm2", [8])

    def yb_rows(i):
        return rows[0:96, :]

    mk_t, mv_t = mk, mv
    sb_ctx = sb("ctxx", rT1, [2, D])

    plan, _ = emit(None)
    _, q = emit(plan)

    with nc.Block() as block:
        @block.sync
        def _(eng):
            q["SP"].replay(eng)
            eng.wait_ge(s_out, 16 * 8)

        @block.scalar
        def _(eng):
            q["AC"].replay(eng)

        @block.vector
        def _(eng):
            q["DV"].replay(eng)

        @block.gpsimd
        def _(eng):
            q["PO"].replay(eng)

        @block.tensor
        def _(eng):
            q["PE"].replay(eng)


_INS = ['x', 'mem', 'norm_mix', 'w_in', 'gmlp_ln_g', 'gmlp_ln_b', 'gmlp_w_s', 'gmlp_b_s', 'cmp_pos', 'cmp_k_w1',
        'cmp_k_w2', 'cmp_v_w1', 'cmp_v_w2', 'w_out', 'norm_xattn', 'norm_mem', 'xattn_wq', 'xattn_wkv', 'xattn_wo',
        'norm_mlp', 'w_up', 'w_down', 'final_norm', 'c_2', 'ctx_2', 'c_ctx_2', 'w_mod_2', 'b_mod_2', 'norm_mix_g_2',
        'norm_ffn_g_2', 'w_in_2', 'hg_lb_2', 'hg_norm_g_2', 'q_norm_g_2', 'k_norm_g_2', 'attn_sink_2', 'w_out_2',
        'w_gate_up_2', 'w_down_2']


def kernel(**inputs):
    from concourse import bacc
    from concourse.bass_utils import run_bass_kernel_spmd

    nc = bacc.Bacc("TRN2", target_bir_lowering=False, num_devices=1)
    arrays, args = {}, {}
    for name in _INS:
        arr = np.ascontiguousarray(inputs[name])
        arrays["in_" + name] = arr
        args[name] = nc.dram_tensor("in_" + name, arr.shape, F, kind="ExternalInput").ap()
    arrays["in_consts"] = constants()
    args["consts"] = nc.dram_tensor("in_consts", (128, NCONST), F, kind="ExternalInput").ap()
    args["out"] = nc.dram_tensor("out_0", (1, S, D), F, kind="ExternalOutput").ap()
    program(nc, args)
    r = run_bass_kernel_spmd(nc, [arrays], core_ids=[0])
    return r.results[0]["out_0"]
```

```python
import numpy as np
import concourse.bass as bass
from concourse import mybir

F = mybir.dt.float32
R = mybir.dt.float32r
ALU = mybir.AluOpType
ACT = mybir.ActivationFunctionType
AX = mybir.AxisListType.X

D = 2048
S = 256
SC = 128.0 ** -0.5
BIG = 3.0e38
EPS = 1e-6
NCH = 2
NRAW, NHI, LOOK = 6, 4, 3
MRATE = 0.62
MR2 = 0.40
FF2 = 5632

MSK, IDN, ONE, LMK, TRL, CMK, RVD, ROC, ROS, HGM, NCONST = (
    0, 896, 1024, 1152, 1408, 1536, 1566, 1568, 1824, 2080, 2852)


def constants():
    c = np.zeros((128, NCONST), np.float32)
    i = np.arange(128)[:, None]
    j = np.arange(128)[None, :]
    neg = np.float32(-1e30)
    c[:, 0:128] = np.where(j >= i, 0, neg)
    c[:, 512:640] = np.where(j <= i, 0, neg)
    c[:, IDN:IDN + 128] = i == j
    c[:, ONE:ONE + 128] = 1.0
    d = 128 + i - np.arange(256)[None, :]
    n = ((d >= 0) & (d <= 128)).astype(int) + ((d >= 0) & (d % 4 == 0)) + ((d >= 0) & (d % 16 == 0))
    c[:, LMK:LMK + 256] = np.where(n > 0, np.log(np.maximum(n, 1)) / SC, neg)
    c[:, TRL:TRL + 128] = i <= j
    for tb in range(2):
        e = np.arange(15)[None, :] * 16 + 31
        ok = e <= i + 128 * tb
        c[:, CMK + 15 * tb:CMK + 15 * tb + 15] = np.where(ok, 0, neg)
        c[:, RVD + tb:RVD + tb + 1] = ok.any(1, keepdims=True)
        t = np.arange(128) + 128 * tb
        f = np.float32(10000.0) ** (-np.arange(32, dtype=np.float32) / np.float32(32))
        for half, pos in ((0, t // 64), (1, t % 64)):
            a = pos.astype(np.float32)[:, None] * f[None, :].astype(np.float32)
            o = 128 * tb + 64 * half
            c[:, ROC + o:ROC + o + 32] = np.cos(a)
            c[:, ROC + o + 32:ROC + o + 64] = np.cos(a)
            c[:, ROS + o:ROS + o + 32] = -np.sin(a)
            c[:, ROS + o + 32:ROS + o + 64] = np.sin(a)
    same = (i // 32) == (j // 32)
    for k, m in enumerate(((i <= j) & same, (i >= j) & same, (i > j) & same, (i < j) & same, i > j, i < j)):
        c[:, HGM + 128 * k:HGM + 128 * k + 128] = m
    c[:, HGM + 768:HGM + 772] = (i // 32) == np.arange(4)[None, :]
    return c


class Queue:

    def __init__(self, sem):
        self.sem, self.n, self.items = sem, 0, []

    def __call__(self, fn, *waits, inc=True):
        self.items.append((list(flat(waits)), fn, self.sem if inc else None, 1))
        if inc:
            self.n += 1
            return (self.sem, self.n)
        return None

    def replay(self, eng):
        seen = {}
        for waits, fn, sem, by in self.items:
            need = {}
            for w in waits:
                need[w[0]] = max(need.get(w[0], 0), w[1])
            for s, v in need.items():
                if seen.get(s, 0) < v:
                    eng.wait_ge(s, v)
                    seen[s] = v
            if fn is not None:
                ins = fn(eng)
                if sem is not None:
                    ins.then_inc(sem, by)


def flat(ws):
    for w in ws:
        if w is None:
            continue
        if isinstance(w, list):
            yield from flat(w)
        else:
            yield w


class Operand:

    def __init__(self, h, l):
        self.h, self.l = h, l
        self.tok = [[] for _ in range(16)]
        self.read = []
        self.pieces = 8
        self.rs = None


class Ring:
    def __init__(self, items):
        self.items = list(items)
        self.free = [[] for _ in items]
        self.order = list(range(len(items)))

    def ready(self):
        return len(self.order) > 0

    def take(self):
        k = self.order.pop(0)
        return k, self.items[k], self.free[k]

    def give(self, k, toks):
        self.free[k] = toks
        self.order.append(k)


def program(nc, a):
    base = [16512]
    top = nc.sbuf_usable_end

    def region(n):
        at = base[0]
        base[0] += n
        assert base[0] <= top, (base[0], top)
        return at

    def sb(name, at, shape, dt=F):
        return nc.alloc_sbuf_tensor_at(name, [128] + list(shape), dt, offset=at)

    rX = region(16384)
    rT1 = region(32768)
    rT2 = region(32768)
    rW = region(4096 * (NRAW + NHI))
    rZ = region(38912)
    rS = region(16384)
    rM = region(8192)
    rG = region(8192)
    rA = region(4096)
    rC = region(4608)
    rY = region(5120)
    rQ = region(4096)

    x = sb("x", rX, [2, D])
    T = {}
    for nm, at in (("1", rT1), ("2", rT2), ("3", rZ)):
        T[nm] = (sb("th" + nm, at, [16, S], R), sb("tl" + nm, at + 16384, [16, S], R))
    raws = [sb(f"raw{i}", rW + 4096 * i, [1024]) for i in range(NRAW)]
    los = [sb(f"wlo{i}", rW + 4096 * i, [1024], R) for i in range(NRAW)]
    his = [sb(f"whi{i}", rW + 4096 * (NRAW + i), [1024], R) for i in range(NHI)]
    stg = [sb(f"stg{i}", rG + 4096 * i, [2, 512]) for i in range(2)]
    acc = [sb(f"acc{i}", (rA if i < 2 else rS + 8192) + 2048 * i, [512]) for i in range(4)]
    mskt = sb("mskt", rC, [896])
    ident = sb("ident", rC + 3584, [128])
    ones = sb("ones", rC + 4096, [128])
    z0 = rZ
    bq = sb("bq", z0, [4, S])
    bk = sb("bk", z0 + 4096, [4, S])
    bv = sb("bv", z0 + 8192, [2, 512])
    cq = sb("cq", z0 + 12288, [8, S])
    cc = sb("cc", z0 + 20480, [4, S])
    ckT = [sb(f"ckT{i}", z0 + 24576 + 4096 * i, [2, S]) for i in range(2)]
    cv = [sb(f"cv{i}", z0 + 26624 + 4096 * i, [2, 256]) for i in range(2)]
    sv = sb("sv", z0 + 32768, [2, 512])
    memx = sb("memx", z0, [2, D])
    xn = sb("xn", rS, [D])
    yb = [sb(f"yb{i}", rS + 8192 + 2048 * i, [512]) for i in range(2)]
    cb = sb("cb", rS, [2, 32, 30])
    Eb = [sb(f"Eb{i}", rS + 2048 * i, [512]) for i in range(3)]
    PTb = [sb(f"PTb{i}", rS + 6144 + 4096 * i, [4, S]) for i in range(2)]
    PCb = [sb(f"PCb{i}", rS + 14336 + 1024 * i, [S]) for i in range(2)]
    mk = sb("mk", rM, [4, S])
    mv = sb("mv", rM + 4096, [2, 512])
    gt = sb("gt", rM, [D])
    lng = sb("lng", rY, [512])
    lnb = sb("lnb", rY + 2048, [512])
    lmk = sb("lmk", rY + 4096, [256])
    ropc = sb("ropc", rY, [2, 128])
    rops = sb("rops", rY + 1024, [2, 128])
    hgm = sb("hgm", rY + 2048, [6, 128])
    q0 = [rQ]

    def small(name, shape):
        n = 4
        for s in shape:
            n *= s
        at = q0[0]
        q0[0] += (n + 31) // 32 * 32
        assert q0[0] <= rQ + 4096 + (top - base[0]), name
        return sb(name, at, shape)

    cols = small("cols", [96])
    cols2 = small("cols2", [69])
    silc = small("silc", [32])
    mod = small("mod", [96])
    modx = small("modx", [32])
    gmod = small("gmod", [2, 16])
    cg = small("cg", [2, 24])
    pc = small("pc", [2, 8, 15])
    cmk = small("cmk", [32])
    hT = small("hT", [2, 32])
    kcT = small("kcT", [32])
    ssp = small("ssp", [2, 4])
    st = small("st", [16])
    sm = small("sm", [96])
    dec = small("dec", [2, 8])
    sink = small("sink", [8])
    ln4 = small("ln4", [8])
    chm = small("chm", [4])
    b2 = rZ
    hK = sb("hK", b2, [2, 512])
    hE1 = [sb(f"hE1{i}", b2 + 4096 + 1024 * i, [S]) for i in range(2)]
    hE2 = [sb(f"hE2{i}", b2 + 6144 + 1024 * i, [S]) for i in range(2)]
    hQs = [sb("hQ0", b2 + 8192, [4, S]), sb("hQ1", rM, [4, S])]
    hVs = [sb("hV0", b2 + 12288, [2, 512]), sb("hV1", rM + 4096, [2, 512])]
    hO = sb("hO", b2 + 16384, [4, S])
    lb = sb("lb", b2 + 20480, [2, 512])
    hST = [sb(f"hST{i}", b2 + 24576 + 1024 * i, [2, 128]) for i in range(2)]
    S0 = sb("S0", b2 + 26624, [16, 128])
    xkT = sb("xkT", b2 + 34816, [2, S])
    xv = sb("xv", b2 + 36864, [2, 256])
    hA = sb("hA", rS, [2, 512])
    hE = sb("hE", rS + 4096, [2, 512])
    hS = [sb("hS0", rS + 8192, [8, 128])]
    hM = [sb(f"hM{i}", rS + 12288 + 2048 * i, [4, 128]) for i in range(2)]
    lkT = sb("lkT", b2, [2, S])
    lv = sb("lv", b2 + 2048, [2, 256])
    lq = sb("lq", b2 + 4096, [8, S])
    rt = sb("rt", b2 + 12288, [2, 512])
    rt2 = sb("rt2", b2 + 16384, [2, 512])
    qkg = sb("qkg", b2 + 20480, [2, 128])
    wk2 = sb("wk2", z0 + 36864, [2, 128])
    vcs = sb("vcs", z0 + 37888, [2, 128])
    wsT = sb("wsT", z0 + 16384, [4, 128])
    wsr = sb("wsr", z0 + 18432, [4, 128])
    trl = sb("trl", z0 + 20480, [128])
    rows = sb("rows", rG, [128])
    rows2 = sb("rows2", rG + 512, [128])
    rows3 = sb("rows3", rG + 1024, [128])

    ps = [nc.alloc_psum_tensor(f"ps{i}", [128, 512], F) for i in range(8)]

    def sem(name):
        return nc.alloc_semaphore(name)

    s_pe, s_act, s_dve, s_pool = sem("s_pe"), sem("s_act"), sem("s_dve"), sem("s_pool")
    s_raw = [sem(f"s_raw{i}") for i in range(NRAW)]
    misc = [sem(f"s_m{i}") for i in range(80)]
    s_out = sem("s_out")

    def emit(plan):
        PE, AC, DV, PO = Queue(s_pe), Queue(s_act), Queue(s_dve), Queue(s_pool)
        SP = Queue(None)
        nm = [0]

        def load(dst, src, *waits, q=None):
            s = misc[nm[0]]
            nm[0] += 1
            (q or SP).items.append((list(flat(waits)), lambda e: e.dma_start(dst, src), s, 16))
            return (s, 16)

        rec = []
        stream = {"next": 0, "dma": 0, "prep": 0, "g": 0, "gn": 0}
        raw_free = {}
        hi_free = {}
        ready = {}

        def issue_dma(upto=None):
            while plan is not None and stream["dma"] < len(plan) and (upto is None or stream["dma"] < upto):
                j = stream["dma"]
                if j >= NRAW and (j - NRAW) not in raw_free:
                    break
                kind, src, shape = plan[j]
                dst = view(raws[j % NRAW], shape)
                SP.items.append((list(flat([raw_free.get(j - NRAW)])), lambda e, dst=dst, src=src: e.dma_start(dst, src),
                                 s_raw[j % NRAW], 16))
                stream["dma"] += 1

        def view(t, shape):
            n = shape[0] * shape[1]
            return t[:, 0:n].rearrange("p (a b) -> p a b", a=shape[0])

        def prepare():
            issue_dma()
            while plan is not None and stream["prep"] < stream["dma"]:
                j = stream["prep"]
                kind, src, shape = plan[j]
                landed = (s_raw[j % NRAW], 16 * (j // NRAW + 1))
                if kind == "m":
                    if not MD["todo"]:
                        break
                    mod_step()
                    issue_dma()
                    continue
                if kind == "r":
                    ready[j] = (landed, None, None, None)
                    stream["prep"] += 1
                    continue
                g = stream["g"]
                if g > stream["gn"] + LOOK:
                    break
                assert g < NHI or g - NHI in hi_free
                used = hi_free.get(g - NHI)
                stream["g"] += 1
                n = shape[0] * shape[1]
                rw, hi, lo = raws[j % NRAW][:, 0:n], his[g % NHI][:, 0:n], los[j % NRAW][:, 0:n]
                th = AC(lambda e, rw=rw, hi=hi: e.activation(hi, rw, ACT.Copy), landed, used)
                tl = DV(lambda e, rw=rw, hi=hi, lo=lo: e.tensor_tensor(lo, rw, hi.bitcast(F), ALU.subtract),
                        landed, th)
                ready[j] = (landed, g, [th, tl], (view(his[g % NHI], shape), view(los[j % NRAW], shape)))
                stream["prep"] += 1

        def chunk(kind, src, shape):
            if plan is None:
                j = len(rec)
                rec.append((kind, src, shape))
                return j, ((s_raw[0], 0), j, None, (view(his[0], shape), view(los[0], shape)))
            if kind == "m":
                j = stream["prep"]
                assert plan[j][0] == kind
                stream["prep"] += 1
                return j, ((s_raw[j % NRAW], 16 * (j // NRAW + 1)), None, None, None)
            while plan[stream["next"]][0] == "m":
                stream["next"] += 1
            j = stream["next"]
            assert plan[j][0] == kind and plan[j][2] == shape
            prepare()
            assert stream["prep"] > j
            stream["next"] += 1
            return j, ready[j]

        RATE = {"big": 1}
        lanes = {"small": [], "big": [], "mod": []}

        def step(name):
            q = lanes[name]
            if q:
                try:
                    next(q[0])
                except StopIteration:
                    q.pop(0)

        def tick():
            step("small")
            for _ in range(RATE["big"]):
                step("big")
            step("mod")
            mods_tick()

        def drain(name):
            while lanes[name]:
                step(name)

        def until(*pairs):
            while any(len(l) < n for l, n in pairs):
                yield

        def after(gen, *pairs, wait=0):
            for _ in range(wait):
                yield
            yield from until(*pairs)
            yield from gen

        def spawn(name, gen):
            lanes[name].append(gen)

        pairs = Ring([(ps[0], ps[1]), (ps[2], ps[3])])
        eb1 = Ring([ps[4]])
        bb = Ring([ps[5], ps[6], ps[7]])

        stgs = Ring(stg)

        class Side:

            def ready(self):
                return eb1.ready() or (not lanes["big"] and bb.ready())

            def take(self):
                r = bb if not lanes["big"] and bb.ready() else eb1
                k, e, fr = r.take()
                return (r, k), e, fr

            def give(self, key, toks):
                key[0].give(key[1], toks)
        eb = Side()

        def gemm(op, w, row0, col0, n, kts, epi, lane="small"):
            while not pairs.ready():
                step("small")
                if not lanes["small"]:
                    step("big")
            k, (p0, p1), freed = pairs.take()
            i, step_n = 0, (NCH if n == 512 else len(kts))
            while i < len(kts):
                m = min(step_n, len(kts) - i)
                r = row0 + 128 * i
                src = w[r:r + 128 * m, col0:col0 + n].rearrange("(a p) n -> p a n", p=128)
                j, (_, g, toks, (wh, wl)) = chunk("g", src, (m, n))
                advance(op, kts[i + m - 1])
                for c in range(m):
                    kt = kts[i + c]
                    first, last = i + c == 0, i + c == len(kts) - 1
                    for tb, p in ((0, p0), (1, p1)):
                        xh = op.h[:, kt, 128 * tb:128 * tb + 128]
                        xl = op.l[:, kt, 128 * tb:128 * tb + 128]
                        trio = ((xh, wh), (xh, wl), (xl, wh))
                        for z, (s, v) in enumerate(trio):
                            end = c == m - 1 and tb == 1 and z == 2
                            t = PE(lambda e, p=p, s=s, v=v, c=c, f=first and z == 0, l=last and z == 2:
                                   e.matmul(p[:, 0:n], s, v[:, c, :], start=f, stop=l),
                                   toks, op.tok[kt], freed if first else None, inc=end)
                hi_free[g] = t
                raw_free[j] = t
                stream["gn"] += 1
                i += m
                tick()
            op.read = [t]

            def release(toks):
                pairs.give(k, toks)
            epi((p0, p1), t, release)
            return t

        def act(out, in_, f, *w, **kw):
            return AC(lambda e: e.activation(out, in_, f, **kw), *w)

        def tt(out, i0, i1, op, *w):
            return DV(lambda e: e.tensor_tensor(out, i0, i1, op), *w)

        def ts(out, i0, s1, s2, o0, o1, *w):
            if o1 is None:
                return DV(lambda e: e.tensor_scalar(out, i0, s1, None, o0), *w)
            return DV(lambda e: e.tensor_scalar(out, i0, s1, s2, o0, o1), *w)

        def copy(out, in_, *w):
            return DV(lambda e: e.tensor_copy(out, in_), *w)

        def recip(out, in_, *w):
            return DV(lambda e: e.reciprocal(out, in_), *w)

        def transpose(out, in_, *w, inc=True, kp=128):
            return PE(lambda e: e.transpose(out, in_, ident[0:kp, 0:kp]), *w, inc=inc)

        def mm(out, l, r, first, last, *w, inc=False):
            return PE(lambda e: e.matmul(out, l, r, start=first, stop=last, skip_group_check=True), *w, inc=inc)

        def split(op, kts, c0, c1, src, *w):
            h, l = op.h[:, kts[0]:kts[-1] + 1, c0:c1], op.l[:, kts[0]:kts[-1] + 1, c0:c1]
            t1 = act(h, src, ACT.Copy, *w)
            t2 = tt(l, src, h.bitcast(F), ALU.subtract, t1, *w)
            for kt in kts:
                op.tok[kt] = op.tok[kt] + [t1, t2]
            return [t1, t2]

        def operand(nm, used):
            op = Operand(*T[nm])
            op.used = used
            return op

        def bc(ap, n):
            return ap.unsqueeze(2).broadcast_to([128, ap.shape[1], n])

        cd = a["consts"]
        t_id = load(ident[:, :], cd[:, IDN:IDN + 128])
        t_r = [load(rows[16 * i:16 * i + 16, :], a[n].rearrange("o (a p) -> (o a) p", p=128))
               for i, n in enumerate(("norm_mix", "norm_xattn", "norm_mem", "norm_mlp", "norm_mix_g_2", "norm_ffn_g_2"))]
        t_r2 = [load(rows2[0:16, :], a["c_2"].rearrange("o (a p) -> (o a) p", p=128)),
                load(rows2[16:32, :], a["c_ctx_2"].rearrange("(a p) -> a p", p=128)),
                load(rows2[32:36, :], a["gmlp_b_s"][0]),
                load(rows2[36:37, :], a["hg_norm_g_2"]),
                load(rows2[37:69, :], a["cmp_pos"][0])]
        w_mod, b_mod = a["w_mod_2"][0], a["b_mod_2"]
        t_b0 = load(rows3[0:96, :], b_mod.rearrange("o (a p) -> (o a) p", p=128))

        t_x0 = {}
        for q in range(4):
            for tb in range(2):
                t_x0[q, tb] = load(memx[:, tb, 512 * q:512 * q + 512],
                                   a["mem"][0, 128 * tb:128 * tb + 128, 512 * q:512 * q + 512])
            issue_dma(q + 1)
        t_c = [load(ones[:, :], cd[:, ONE:ONE + 128]), load(mskt[:, :], cd[:, 0:896])]
        issue_dma()
        k, e0, _ = eb.take()
        transpose(e0[:, 0:96], rows[0:96, :], t_id, t_r, kp=96, inc=False)
        transpose(e0[:, 128:197], rows2[0:69, :], t_r2, kp=69, inc=False)
        t = transpose(e0[:, 256:352], rows3[0:96, :], t_b0, kp=96)
        t_cols = copy(cols[:, :], e0[:, 0:96], t)
        t_cols2 = copy(cols2[:, :], e0[:, 128:197], t)
        t_bm = copy(bmc[:, :], e0[:, 256:352], t)
        eb.give(k, [t_cols, t_cols2, t_bm])
        stgs.free = [[t], [t]]
        t_sil = act(silc[:, :], cols2[:, 0:32], ACT.Silu, t_cols2)
        gain = {n: cols[:, 16 * i:16 * i + 16] for i, n in enumerate(("mix", "xa", "mem", "mlp", "mix2", "ffn2"))}
        bsT, hgn, posT = cols2[:, 32:36], cols2[:, 36:37], cols2[:, 37:69]

        MD = {"todo": [], "credit": 0.0, "rate": 0.0, "acc": [None] * 4, "done": [], "gt": [], "xdone": [], "cur": None}

        def mod_step():
            j, kc, dest = MD["todo"].pop(0)
            both = j < 8
            if kc == 0:
                used = [j % 2, 2 + j % 2] if both else [j % 2]
                if any(isinstance(MD["acc"][v], tuple) and MD["acc"][v][0] == "late" for v in used):
                    drain_mod_sums()
                MD["cur"] = [(v, MD["acc"][v]) for v in used]
            src = w_mod[256 * kc:256 * kc + 256, 512 * j:512 * j + 512].rearrange("(a p) n -> p a n", p=128)
            jj, (landed, _, _, _) = chunk("m", src, (NCH, 512))
            rv = view(raws[jj % NRAW], (NCH, 512))
            for c in range(NCH):
                nxt = []
                for i, (v, t) in enumerate(MD["cur"]):
                    col = 16 * i + NCH * kc + c
                    sc = silc[:, col:col + 1]
                    first = kc == 0 and c == 0

                    def piece(e, v=v, c=c, sc=sc, rv=rv, first=first):
                        if first:
                            return e.tensor_scalar(acc[v][:, :], rv[:, c, :], sc, None, ALU.mult)
                        return e.scalar_tensor_tensor(out=acc[v][:, :], in0=rv[:, c, :], scalar=sc, in1=acc[v][:, :],
                                                      op0=ALU.mult, op1=ALU.add)
                    nxt.append((v, DV(piece, landed, t, t_sil)))
                MD["cur"] = nxt
            raw_free[jj] = [t for _, t in MD["cur"]]
            if kc == 7:
                spawn("mod", mod_sum(j, dest, MD["cur"]))
                for v, _ in MD["cur"]:
                    MD["acc"][v] = ("late", j)

        def drain_mod_sums():
            while lanes["mod"]:
                if not eb.ready():
                    step("small")
                step("mod")

        def mod_sum(j, dest, cur):
            for _ in range(LOOK):
                yield
            while not eb.ready():
                yield
            k, e, fr = eb.take()
            for i, (v, ta) in enumerate(cur):
                for q in range(4):
                    t = mm(e[:, 4 * i + q:4 * i + q + 1], acc[v][:, 128 * q:128 * q + 128], ones[:, 0:1],
                           True, True, fr, ta, inc=(i == len(cur) - 1 and q == 3))
            t1 = tt(mod[:, 4 * j:4 * j + 4], e[:, 0:4], bmc[:, 4 * j:4 * j + 4], ALU.add, t, t_bm)
            MD["done"].append(t1)
            outs = [t1]
            if len(cur) > 1:
                t2 = tt(modx[:, 4 * j:4 * j + 4], e[:, 4:8], bmc[:, 4 * j:4 * j + 4], ALU.add, t, t_bm)
                MD["xdone"].append(t2)
                outs.append(t2)
            eb.give(k, outs)
            for v, _ in cur:
                MD["acc"][v] = t

        def mods_tick():
            if plan is not None or not MD["todo"]:
                return
            MD["credit"] += MD["rate"]
            while MD["credit"] >= 1 and MD["todo"]:
                MD["credit"] -= 1
                mod_step()

        def mods_start(j0, j1, dest, rate):
            mods_finish()
            MD["todo"] += [(j, kc, dest) for j in range(j0, j1) for kc in range(8)]
            MD["rate"], MD["credit"] = rate, 0.0

        def mods_more(j0, j1):
            MD["todo"] += [(j, kc, "col") for j in range(j0, j1) for kc in range(8)]

        def mods_finish():
            while MD["todo"]:
                n = len(MD["todo"])
                if plan is None:
                    mod_step()
                else:
                    prepare()
                assert len(MD["todo"]) < n
            drain_mod_sums()

        def rstd_of(ss, n, out, *w):
            t1 = ts(out, ss, 1.0 / n, EPS, ALU.mult, ALU.add, *w)
            t2 = act(out, out, ACT.Sqrt, t1)
            return recip(out, out, t2)

        XN = {"free": [[], [], [], []], "yb": [[], []], "n": 0}

        def turn(src, srct, rs, op, g, sh, gtok, used, rest=0, ease=False):
            pieces = [(q, tb) for q in range(4) for tb in range(2)]
            made = {}

            def scale(i):
                if i < 8 and i not in made:
                    q, tb = pieces[i]
                    v = XN["n"] % 4
                    XN["n"] += 1
                    xp = xn[:, 512 * v:512 * v + 512]
                    made[i] = (v, xp, act(xp, src[:, tb, 512 * q:512 * q + 512], ACT.Copy,
                                          srct(q, tb), rs[tb][1], XN["free"][v], scale=rs[tb][0]))

            def run():
                if rs is not None:
                    scale(0)
                    scale(1)
                    if ease:
                        yield
                        yield
                for j, (q, tb) in enumerate(pieces):
                    if rs is not None:
                        scale(j + 2)
                        v, xp, t_n = made[j]
                    else:
                        if src is x and RES["n"] <= q:
                            while RES["n"] <= q:
                                yield
                            yield
                        v, xp, t_n = None, src[:, tb, 512 * q:512 * q + 512], srct(q, tb)
                    ring = bb if bb.ready() else eb
                    while not ring.ready():
                        yield
                    k, e, fr = ring.take()
                    for i in range(4):
                        t = transpose(e[:, 128 * i:128 * i + 128], xp[:, 128 * i:128 * i + 128],
                                      t_n, fr, inc=(i == 3))
                    if v is not None:
                        XN["free"][v] = [t]
                    elif src is x:
                        RES["tok"][2 * q + tb] = RES["tok"][2 * q + tb] + [t]
                    u = j % 2
                    ev = e[:, :].rearrange("p (a b) -> p a b", a=4)
                    yv = yb[u][:, :].rearrange("p (a b) -> p a b", a=4)
                    t1 = tt(yv, ev, bc(g[:, 4 * q:4 * q + 4], 128), ALU.mult, t, gtok, XN["yb"][u])
                    ring.give(k, [t1])
                    if sh is not None:
                        t1 = tt(yv, yv, bc(sh[:, 4 * q:4 * q + 4], 128), ALU.add, t1, gtok)
                    XN["yb"][u] = split(op, list(range(4 * q, 4 * q + 4)), 128 * tb, 128 * tb + 128, yv, t1, used)
                    op.pieces = j + 1
                    yield
                    for _ in range(rest):
                        yield
            op.pieces = 0
            op.gen = run()
            return op.gen

        def advance(op, kt):
            while op.pieces < 2 * (min(kt, 15) // 4 + 1):
                next(op.gen)

        def stats(src, tok, dst):
            out = []
            for tb in range(2):
                t1 = act(xn[:, :], src[:, tb, :], ACT.Square, tok, XN["free"], accum_out=dst[:, tb:tb + 1])
                XN["free"] = [[t1] for _ in range(4)]
                out.append(t1)
            t = rstd_of(dst, D, dst, out)
            return [(dst[:, tb:tb + 1], t) for tb in range(2)]

        def sums(dst, toks):
            t1 = DV(lambda e: e.tensor_reduce(dst, ssp[:, :, :], AX, ALU.add), toks)
            t = rstd_of(dst, D, dst, t1)
            return [(dst[:, tb:tb + 1], t) for tb in range(2)]

        def scaled(by, tb):
            if by is None:
                return {}, None
            return dict(scale=by.rs[tb][0]), by.rs[tb][1]

        def to_heads(dst, h0, f=ACT.Copy, used=(), done=None, nh=4, by=None):
            def epi(p, t, release):
                def run():
                    while not stgs.ready():
                        yield
                    k, sg, fr = stgs.take()
                    w = 128 * nh
                    kw, tr = scaled(by, 0)
                    t0 = act(sg[:, 0, 0:w], p[0][:, 0:w], ACT.Copy, t, fr, tr, **kw)
                    if by is None:
                        t1 = copy(sg[:, 1, 0:w], p[1][:, 0:w], t, fr)
                    else:
                        t1 = ts(sg[:, 1, 0:w], p[1][:, 0:w], by.rs[1][0], None, ALU.mult, None, t, fr, by.rs[1][1])
                    release([t0, t1])
                    yield
                    yield
                    out = []
                    for i in range(0, nh, 2):
                        while not eb.ready():
                            yield
                        kb, e, fb = eb.take()
                        for h in range(2):
                            for tb in range(2):
                                t2 = transpose(e[:, 256 * h + 128 * tb:256 * h + 128 * tb + 128],
                                               sg[:, tb, 128 * (i + h):128 * (i + h) + 128], t0, t1, fb,
                                               inc=(h == 1 and tb == 1))
                        t3 = act(dst[:, h0 + i:h0 + i + 2, :], e[:, :].rearrange("p (a b) -> p a b", a=2), f, t2, list(used))
                        eb.give(kb, [t3])
                        out.append(t3)
                        yield
                    stgs.give(k, [t2])
                    if done is not None:
                        done.extend(out)
                spawn("small", run())
            return epi

        def to_rows(dst, c0, n, s0, f, used, done, by=None):
            def epi(p, t, release):
                o = [act(dst[:, tb, c0:c0 + n], p[tb][:, s0:s0 + n], f, t, list(used), scaled(by, tb)[1],
                         **scaled(by, tb)[0]) for tb in range(2)]
                done.extend(o)
                release(o)
            return epi

        def two(e1, e2):
            def epi(p, t, release):
                got = []

                def one(toks):
                    got.append(toks)
                    if len(got) == 2:
                        release(got[0] + got[1])
                e2(p, t, one)
                e1(p, [t, got[0]], one)
            return epi

        RES = {"w": [None] * 8, "tok": [], "ss": [], "n": 4}

        def residual(n, last, scale=None, out=None):
            def epi(p, t, release):
                o = []
                for tb in range(2):
                    xs = x[:, tb, 512 * n:512 * n + 512]
                    i = 2 * n + tb
                    if scale is None:
                        t1 = tt(xs, p[tb][:, :], xs, ALU.add, t, RES["tok"][i])
                        o.append(t1)
                    else:
                        while len(MD["gt"]) < 4 or not stgs.ready():
                            step("small")
                        k, sg, fr = stgs.take()
                        t0 = tt(sg[:, 0, :], p[tb][:, :], scale[:, 512 * n:512 * n + 512], ALU.mult, t, fr, MD["gt"])
                        o.append(t0)
                        t1 = tt(xs, sg[:, 0, :], xs, ALU.add, t0, RES["tok"][i])
                        stgs.give(k, [t1])
                    RES["tok"][i] = [t1]
                    RES["w"][i] = [t1]
                    if last:
                        t2 = act(yb[tb][:, :], xs, ACT.Square, t1, XN["yb"][tb], accum_out=ssp[:, tb, n:n + 1])
                        XN["yb"][tb] = [t2]
                        RES["ss"].append(t2)
                        RES["tok"][i] = [t1, t2]
                        RES["n"] = n + 1
                    if out is not None:
                        SP.items.append(([t1], lambda e, tb=tb, xs=xs: e.dma_start(
                            out[0, 128 * tb:128 * tb + 128, 512 * n:512 * n + 512], xs), s_out, 16))
                release(o)
            return epi

        def attention(nh, q, parts, op, kt0, used, qtok, post=None, snk=None, extra=None, fac=None):
            ER = Ring(Eb)
            PR = Ring(PTb)
            CR = Ring(PCb)
            for r in (ER, PR, CR):
                r.free = [[z["end"] if isinstance(z, dict) else z for z in used["scr"]] for _ in r.items]
            st8 = {"sm": 0}
            heads = {}
            smfree = [None] * 8

            def s1(u):
                h, tb = u["h"], u["tb"]
                u["bk"], bank, fr = bb.take()
                u["bank"] = bank
                last = [(p, z) for p in parts for z in p["k"](h, tb)]
                for i, (p, (kap, col)) in enumerate(last):
                    n = kap.shape[1]
                    u["t"] = mm(bank[:, col:col + n], q(h, tb), kap, True, True, fr, qtok, p["tok"],
                                inc=(i == len(last) - 1))

            def s2(u):
                h, tb = u["h"], u["tb"]
                i = (2 * h + tb) % 8
                sb8 = sm[:, 12 * i:12 * i + 12]
                u["s"] = sb8
                u["e"], E, fr = ER.take()
                u["E"] = E
                tks = []
                for j, p in enumerate(parts):
                    o, n = p["off"], p["n"](tb)
                    t = DV(lambda e, o=o, n=n, p=p, j=j, E=E, bank=u["bank"]: e.tensor_tensor_reduce(
                        E[:, o:o + n], bank[:, o:o + n], p["mask"](tb), -SC, BIG, ALU.add, ALU.min,
                        sb8[:, j:j + 1]), u["t"], fr, smfree[i])
                    tks.append(t)
                bb.give(u["bk"], tks)
                ex = []
                if snk is not None:
                    t = DV(lambda e: e.tensor_tensor(sb8[:, 0:1], sb8[:, 0:1], snk[1][:, h:h + 1], ALU.min), tks[0], snk[2])
                    tks[0] = t
                    ex.append(act(sb8[:, 8:9], snk[0][:, h:h + 1], ACT.Exp, t, bias=sb8[:, 0:1]))
                out = []
                for j, p in enumerate(parts):
                    o, n = p["off"], p["n"](tb)
                    out.append(act(E[:, o:o + n], E[:, o:o + n], ACT.Exp, tks[j], scale=-1.0, bias=sb8[:, j:j + 1],
                                   accum_out=sb8[:, 2 + j:3 + j]))
                if snk is not None:
                    out.append(tt(sb8[:, 2:3], sb8[:, 2:3], sb8[:, 8:9], ALU.add, out[0], ex))
                np_ = len(parts)
                t = recip(sb8[:, 4:4 + np_], sb8[:, 2:2 + np_], out)
                if post is not None:
                    t = tt(sb8[:, 4:4 + np_], sb8[:, 4:4 + np_], post[0](h, tb), ALU.mult, t, post[1])
                u["n"] = []
                for j, p in enumerate(parts):
                    o, n = p["off"], p["n"](tb)
                    u["n"].append(ts(E[:, o:o + n], E[:, o:o + n], sb8[:, 4 + j:5 + j], None, ALU.mult, None, t))
                smfree[i] = u["n"]

            def s25(u):
                h, tb = u["h"], u["tb"]
                if tb or extra is None:
                    return
                H = heads.setdefault(h, {})
                kb, bank, fr = eb.take()
                H["ck"], H["PC"], f2 = CR.take()
                for z in range(2):
                    t = transpose(bank[0:15, 256 + 128 * z:384 + 128 * z], pc[:, z, h, :], extra["tok"], fr, inc=(z == 1))
                H["tcp"] = act(H["PC"][0:15, :], bank[0:15, 256:512], ACT.Copy, t, f2)
                eb.give(kb, [H["tcp"]])

            def s3(u):
                h, tb = u["h"], u["tb"]
                if tb == 0:
                    k1, PT, f1 = PR.take()
                    heads.setdefault(h, {}).update(k=k1, PT=PT, fr=f1, toks=[])
                H = heads[h]
                kb, bank, fr = bb.take()
                blocks = []
                for p in parts:
                    for b in range(p["nkb"](tb)):
                        blocks.append((p["slot"] + b, p["off"] + 128 * b))
                for i, (slot, c) in enumerate(blocks):
                    t = transpose(bank[:, 128 * slot:128 * slot + 128], u["E"][:, c:c + 128], u["n"], fr,
                                  inc=(i == len(blocks) - 1))
                ER.give(u["e"], [t])
                dst = H["PT"][:, :, 128 * tb:128 * tb + 128]
                src = bank[:, :].rearrange("p (a b) -> p a b", a=4)
                if len(blocks) == 4:
                    tc = act(dst, src, ACT.Copy, t, H["fr"])
                else:
                    step_ = blocks[1][0] - blocks[0][0] if len(blocks) > 1 else 1
                    sl = slice(blocks[0][0], blocks[-1][0] + 1, step_)
                    tc = act(dst[:, sl, :], src[:, sl, :], ACT.Copy, t, H["fr"])
                bb.give(kb, [tc])
                H["toks"].append(tc)

            def s4(u):
                h, tb = u["h"], u["tb"]
                if tb == 0:
                    return
                H = heads[h]
                ring = eb1 if eb1.ready() else bb
                kb, bank, fr = ring.take()
                ops = []
                for p in parts:
                    for b in range(p["nkb"](1)):
                        lo = 0 if b < p["nkb"](0) else 128
                        ops.append((p["v"](h, b), H["PT"][:, p["slot"] + b, lo:S], lo, p["vtok"]))
                tcp = H.get("tcp")
                for i, (v, pt, lo, vt) in enumerate(ops):
                    t = mm(bank[:, lo:S], v, pt, i == 0, extra is None and i == len(ops) - 1, H["toks"], fr, vt, tcp,
                           inc=(extra is None and i == len(ops) - 1))
                if extra is not None:
                    t = mm(bank[:, 0:S], vcs[0:15, h // 4, :], H["PC"][0:15, :], False, True, tcp, extra["vtok"], inc=True)
                    CR.give(H["ck"], [t])
                PR.give(H["k"], [t])
                tk = split(op, [kt0 + h], 0, S, bank[:, 0:S].unsqueeze(1), t, used["op"])
                ring.give(kb, tk)

            units = [dict(h=h, tb=tb) for h in range(nh) for tb in range(2)]
            n = len(units)
            for i in range(n + 4):
                for d, f in ((4, s4), (3, s3), (2, s25), (1, s2), (0, s1)):
                    if 0 <= i - d < n:
                        f(units[i - d])
                yield
            used["end"] = [r for r in (ER.free + PR.free + CR.free)]

        def late_loads():
            nonlocal t_cst, t_ln, t_ws, t_w2, t_sink
            t_cst = [load(lmk[:, :], cd[:, LMK:LMK + 256]), load(trl[:, :], cd[:, TRL:TRL + 128]),
                     load(cmk[:, :], cd[:, CMK:CMK + 32])]
            t_ln = [load(lng[:, :], a["gmlp_ln_g"].broadcast_to([128, 512])),
                    load(lnb[:, :], a["gmlp_ln_b"].broadcast_to([128, 512]))]
            t_ws = load(wsr[:, :, :], a["gmlp_w_s"][0].rearrange("g t s -> t g s"))
            t_w2 = [load(wk2[:, 0, :], a["cmp_k_w2"][0]), load(wk2[:, 1, :], a["cmp_v_w2"][0])]
            t_sink = load(sink[:, :], a["attn_sink_2"].broadcast_to([128, 8]))

        t_cst = t_ln = t_ws = t_w2 = t_sink = None
        op2 = operand("2", [])
        turn(memx, lambda q, tb: t_x0[q, tb], None, op2, gain["mem"], None, t_cols, [])
        for _ in range(3):
            next(op2.gen)
        lanes["small"].append(op2.gen)

        def load_x():
            for q in range(4):
                for tb in range(2):
                    RES["tok"].append([load(x[:, tb, 512 * q:512 * q + 512],
                                            a["x"][0, 128 * tb:128 * tb + 128, 512 * q:512 * q + 512])])
                yield
            late_loads()
            op2.rs = stats(memx, list(t_x0.values()), st[:, 0:2])
        spawn("mod", load_x())

        def start_x():
            while lanes["mod"]:
                step("mod")
            advance(op2, 15)
            op1.rs = stats(x, list(RES["tok"]), st[:, 2:4])
            turn(x, lambda q, tb: RES["tok"][2 * q + tb], None, op1, gain["mix"], None, t_cols, [])
            lanes["small"].append(op1.gen)
        op1 = operand("1", [])

        w_in, w_kv = a["w_in"][0], a["xattn_wkv"][0]
        t_mk, t_mv = [], []
        gemm(op2, w_kv, 0, 0, 512, range(16), to_heads(mk_t, 0, used=[], done=t_mk, by=op2))
        start_x()
        gemm(op2, w_kv, 0, 512, 512, range(16), to_rows(mv_t, 0, 512, 0, ACT.Copy, [], t_mv, by=op2))

        k, e0, fr = eb.take()
        for g in range(4):
            t = transpose(e0[:, 128 * g:128 * g + 128], wsr[:, g, :], t_ws, fr, inc=(g == 3))
        t_wsT = tt(wsT[:, :, :], e0[:, :].rearrange("p (a b) -> p a b", a=4),
                   trl[:, :].unsqueeze(1).broadcast_to([128, 4, 128]), ALU.mult, t, t_cst)
        eb.give(k, [t_wsT])

        mods_start(8, 20, "col", MRATE)
        tq, tk_, tv_ = [], [], []
        gemm(op1, w_in, 0, 1024, 512, range(16), to_heads(bq, 0, done=tq, by=op1))
        gemm(op1, w_in, 0, 1536, 512, range(16), to_heads(bk, 0, done=tk_, by=op1))
        gemm(op1, w_in, 0, 2048, 512, range(16), to_rows(bv, 0, 512, 0, ACT.Copy, [], tv_, by=op1))

        t_sv = []

        def epi_v(p, t, release):
            def run():
                while not stgs.ready():
                    yield
                k, sg, fr = stgs.take()
                t0 = [act(sg[:, tb, :], p[tb][:, :], ACT.Gelu_apprx_tanh, t, fr, op1.rs[tb][1], scale=op1.rs[tb][0],
                          accum_out=ln4[:, tb:tb + 1]) for tb in range(2)]
                release(t0)
                yield
                tn, t3 = [], []
                for tb in range(2):
                    m, v = ln4[:, tb:tb + 1], ln4[:, 2 + tb:3 + tb]
                    t1 = ts(m, m, 1.0 / 512, None, ALU.mult, None, t0[tb])
                    t2 = ts(sg[:, tb, :], sg[:, tb, :], m, None, ALU.subtract, None, t1)
                    t3.append(act(sv[:, tb, :], sg[:, tb, :], ACT.Square, t2, accum_out=v))
                yield
                t4 = rstd_of(ln4[:, 2:4], 512, ln4[:, 2:4], t3)
                for tb in range(2):
                    v = ln4[:, 2 + tb:3 + tb]
                    t5 = DV(lambda e, tb=tb, v=v: e.scalar_tensor_tensor(
                        out=sg[:, tb, :], in0=sg[:, tb, :], scalar=v, in1=lng[:, :], op0=ALU.mult, op1=ALU.mult),
                        t4, t_ln)
                    tn.append(tt(sg[:, tb, :], sg[:, tb, :], lnb[:, :], ALU.add, t5))
                    yield
                for tb in range(2):
                    while not eb.ready():
                        yield
                    kb, e, fb = eb.take()
                    for g in range(4):
                        t6 = mm(e[:, 128 * g:128 * g + 128], wsT[:, g, :], sg[:, tb, 128 * g:128 * g + 128],
                                True, True, tn[tb], fb, t_wsT, inc=(g == 3))
                    t7 = tt(sv[:, tb, :].rearrange("p (a b) -> p a b", a=4), e[:, :].rearrange("p (a b) -> p a b", a=4),
                            bc(bsT, 128), ALU.add, t6, t_cols2)
                    eb.give(kb, [t7])
                    t_sv.append(t7)
                    yield
                stgs.give(k, [t6])
            spawn("small", run())

        op2m = operand("2", [])

        def epi_u(p, t, release):
            def run():
                while not stgs.ready():
                    yield
                k, sg, fr = stgs.take()
                t0 = [act(sg[:, tb, :], p[tb][:, :], ACT.Gelu_apprx_tanh, t, fr, op1.rs[tb][1], scale=op1.rs[tb][0])
                      for tb in range(2)]
                release(t0)
                t1 = tt(sg[:, :, :], sg[:, :, :], sv[:, :, :], ALU.mult, t0, t_sv)
                yield
                for i in range(0, 4, 2):
                    while not eb.ready():
                        yield
                    kb, e, fb = eb.take()
                    for h in range(2):
                        for tb in range(2):
                            t2 = transpose(e[:, 256 * h + 128 * tb:256 * h + 128 * tb + 128],
                                           sg[:, tb, 128 * (i + h):128 * (i + h) + 128], t1, fb, inc=(h == 1 and tb == 1))
                    eb.give(kb, split(op2m, [i, i + 1], 0, S, e[:, :].rearrange("p (a b) -> p a b", a=2), t2, op2.read))
                    yield
                stgs.give(k, [t2])
            spawn("small", run())


        use = {"scr": [XN["free"], XN["yb"]], "op": op2.read}
        tri = lambda tb: (lmk[:, 128:256] if tb == 0 else lmk[:, 0:256])
        spawn("big", after(attention(
            4, lambda h, tb: bq[:, h, 128 * tb:128 * tb + 128],
            [dict(k=lambda h, tb: [(bk[:, h, 0:128 * tb + 128], 0)], off=0, n=lambda tb: 128 * tb + 128, mask=tri,
                  slot=0, v=lambda h, b: bv[:, b, 128 * h:128 * h + 128], nkb=lambda tb: tb + 1,
                  tok=[tk_, t_cst], vtok=tv_)], op2m, 4, use, tq), (tq, 2), (tk_, 2), (tv_, 2)))

        gemm(op1, w_in, 0, 512, 512, range(16), epi_v)
        gemm(op1, w_in, 0, 0, 512, range(16), epi_u)
        t_cc, t_cq, t_ck, t_cv = [], [], [[], []], [[], []]
        gemm(op1, w_in, 0, 3584, 512, range(16), to_heads(cc, 0, done=t_cc, by=op1))

        t_cb = []
        t_h = []

        def compress():
            yield from until((t_cc, 2))
            for m in range(2):
                for g in range(2):
                    src = cc[:, 2 * m + g, :]
                    for half in range(2):
                        i0 = src[:, 16 * half:16 * half + 240].rearrange("p (n l) -> p l n", l=16)
                        t_cb.append(tt(cb[:, m, 16 * half:16 * half + 16, 15 * g:15 * g + 15], i0,
                                       bc(posT[:, 16 * half:16 * half + 16], 15), ALU.add, t_cc, t_cols2, use["end"]))
            yield
            yield
            for m, w1 in ((0, a["cmp_k_w1"][0]), (1, a["cmp_v_w1"][0])):
                k, e, fr = bb.take()
                for c in range(4):
                    src = w1[1024 * c:1024 * c + 1024, :].rearrange("(l d) o -> d l o", d=128)
                    j, (landed, _, _, _) = chunk("r", src, (8, 128))
                    rv = view(raws[j % NRAW], (8, 128))
                    for l in range(8):
                        t = mm(e[:, 0:30], rv[:, l, :], cb[:, m, 8 * c + l, :], c == 0 and l == 0, c == 3 and l == 7,
                               landed, t_cb, fr, inc=(l == 7))
                    raw_free[j] = t
                    yield
                t1 = act(hT[:, m, 0:30], e[:, 0:30], ACT.Gelu_apprx_tanh, t)
                t_h.append(t1)
                bb.give(k, [t1])
                yield
            k, e, fr = bb.take()
            mm(e[:, 0:30], wk2[:, 0, :], hT[:, 0, 0:30], True, True, t_h, t_w2, fr)
            for g in range(2):
                t = mm(e[0:15, 128 + 128 * g:256 + 128 * g], hT[:, 1, 15 * g:15 * g + 15], wk2[:, 1, :], True, True,
                       inc=(g == 1))
            t1 = copy(kcT[:, 0:30], e[:, 0:30], t)
            t2 = copy(vcs[0:15, :, :], e[0:15, 128:384].rearrange("p (a b) -> p a b", a=2), t)
            bb.give(k, [t1, t2])
            t_h.extend([t1, t2])

        spawn("big", compress())
        gemm(op1, w_in, 0, 2560, 512, range(16), to_heads(cq, 0, done=t_cq, by=op1))
        gemm(op1, w_in, 0, 3072, 512, range(16), to_heads(cq, 4, done=t_cq, by=op1))
        for i in range(2):
            gemm(op1, w_in, 0, 4096 + 512 * i, 512, range(16),
                 two(to_heads(ckT[i], 0, done=t_ck[i], nh=2, by=op1), to_rows(cv[i], 0, 256, 256, ACT.Copy, [], t_cv[i], by=op1)))
        t_cg = []
        gemm(op1, w_in, 0, 5120, 24, range(16), to_rows(cg, 0, 24, 0, ACT.Sigmoid, [], t_cg, by=op1))
        t_op1 = op1.read

        t_pc = []
        def probabilities():
            yield from until((t_cq, 4), (t_cg, 2), (t_ck[0], 1), (t_ck[1], 1))
            for tb in range(2):
                k, e, fr = bb.take()
                for h in range(8):
                    t = mm(e[:, 15 * h:15 * h + 15], cq[:, h, 128 * tb:128 * tb + 128], kcT[:, 15 * (h // 4):15 * (h // 4) + 15],
                           True, True, t_cq, t_h, fr, inc=(h == 7))
                P = pc[:, tb, :, :]
                m8 = sm[:, 8 * tb:8 * tb + 8]
                d8 = sm[:, 16 + 8 * tb:24 + 8 * tb]
                t1 = tt(P, e[:, 0:120].rearrange("p (a b) -> p a b", a=8),
                        cmk[:, 15 * tb:15 * tb + 15].unsqueeze(1).broadcast_to([128, 8, 15]), ALU.add, t, t_cst)
                bb.give(k, [t1])
                t2 = DV(lambda e, P=P, m8=m8: e.tensor_reduce(m8, P, AX, ALU.max), t1, use["end"])
                t3 = tt(P, P, bc(m8, 15), ALU.subtract, t2)
                t4 = act(P, P, ACT.Exp, t3, scale=SC)
                t5 = DV(lambda e, P=P, d8=d8: e.tensor_reduce(d8, P, AX, ALU.add), t4)
                t6 = recip(d8, d8, t5)
                gv = cg[:, tb, :].rearrange("p (h j) -> p h j", j=3)
                t7 = DV(lambda e, d8=d8, gv=gv, tb=tb: e.scalar_tensor_tensor(
                    out=d8, in0=d8, scalar=cmk[:, 30 + tb:31 + tb], in1=gv[:, :, 0], op0=ALU.mult, op1=ALU.mult), t6, t_cg)
                t_pc.append(tt(P, P, bc(d8, 15), ALU.mult, t7))
                yield

        spawn("big", probabilities())
        cmask = lambda tb: (mskt[:, 512:640] if tb == 0 else mskt[:, 384:640])
        use2 = {"scr": [use, t_h, t_pc], "op": op2.read}
        cparts = [dict(k=lambda h, tb, i=i: [(ckT[i][:, h // 4, 0:128 * tb + 128], 256 * i)], off=256 * i,
                       n=lambda tb: 128 * tb + 128, mask=cmask, slot=2 * i,
                       v=lambda h, b, i=i: cv[i][:, b, 128 * (h // 4):128 * (h // 4) + 128],
                       nkb=lambda tb: tb + 1, tok=[t_ck[i], t_c], vtok=t_cv[i]) for i in range(2)]
        spawn("big", attention(
            8, lambda h, tb: cq[:, h, 128 * tb:128 * tb + 128], cparts, op2m, 8, use2, t_cq,
            post=(lambda h, tb: cg[:, tb, 3 * h + 1:3 * h + 3], t_cg), extra={"tok": t_pc, "vtok": t_h}))
        w_out = a["w_out"][0]
        for n in range(4):
            gemm(op2m, w_out, 0, 512 * n, 512, range(8), residual(n, False))
        drain("big")
        XN["free"] = [[use2["end"]] for _ in range(4)]
        XN["yb"] = [[use2["end"]], [use2["end"]]]
        def early_turn(nm, used, g):
            RES["n"] = 0
            op = operand(nm, used)
            turn(x, lambda q, tb: RES["w"][2 * q + tb], None, op, g, None, t_cols, used)
            lanes["small"].append(op.gen)
            return op

        def early_rs(op, dst):
            op.rs = sums(dst, RES["ss"])
            RES["ss"] = []

        opx = early_turn("1", t_op1, gain["xa"])
        for n in range(4):
            gemm(op2m, w_out, 1024, 512 * n, 512, range(8, 16), residual(n, True))

        def norm_turn(nm, used, g, sh=None, gtok=None):
            rs = sums(st[:, 14:16], RES["ss"])
            RES["ss"] = []
            op = operand(nm, used)
            toks = [list(t) for t in RES["tok"]]
            turn(x, lambda q, tb: toks[2 * q + tb], rs, op, g, sh, gtok or t_cols, used)
            for _ in range(3):
                next(op.gen)
            lanes["small"].insert(0, op.gen)
            return op

        early_rs(opx, st[:, 4:6])
        xq_t = []
        gemm(opx, a["xattn_wq"][0], 0, 0, 512, range(16), to_heads(bq, 0, used=[use2["end"]], done=xq_t, by=opx))
        drain("small")
        zero = lambda tb: mskt[:, 128:384]
        use3 = {"scr": [XN["free"], XN["yb"]], "op": op2m.read}
        opo = operand("2", [])
        spawn("big", attention(
            4, lambda h, tb: bq[:, h, 128 * tb:128 * tb + 128],
            [dict(k=lambda h, tb: [(mk[:, h, :], 0)], off=0, n=lambda tb: 256, mask=zero, slot=0,
                  v=lambda h, b: mv[:, b, 128 * h:128 * h + 128], nkb=lambda tb: 2, tok=[t_mk, t_c], vtok=t_mv)],
            opo, 0, use3, xq_t))
        drain("big")
        XN["free"] = [[use3["end"]] for _ in range(4)]
        XN["yb"] = [[use3["end"]], [use3["end"]]]
        opm = early_turn("1", opx.read, gain["mlp"])
        MD["rate"] = 0.0
        for n in range(4):
            gemm(opo, a["xattn_wo"][0], 0, 512 * n, 512, range(4), residual(n, True))

        early_rs(opm, st[:, 12:14])

        def hidden(op, kt, used, fn):
            def epi(p, t, release):
                def run():
                    while not stgs.ready():
                        yield
                    k, sg, fr = stgs.take()
                    t1 = fn(p, t, sg, fr, release)
                    yield
                    yield
                    for i in range(0, 4, 2):
                        while not eb.ready():
                            yield
                        kb, e, fb = eb.take()
                        for h in range(2):
                            for tb in range(2):
                                t2 = transpose(e[:, 256 * h + 128 * tb:256 * h + 128 * tb + 128],
                                               sg[:, tb, 128 * (i + h):128 * (i + h) + 128], t1, fb,
                                               inc=(h == 1 and tb == 1))
                        eb.give(kb, split(op, [kt + i, kt + i + 1], 0, S,
                                          e[:, :].rearrange("p (a b) -> p a b", a=2), t2, used))
                        yield
                    stgs.give(k, [t2])
                spawn("small", run())
            return epi

        def relu2(p, t, sg, fr, release):
            t0 = [act(sg[:, tb, :], p[tb][:, :], ACT.Relu, t, fr, opm.rs[tb][1], scale=opm.rs[tb][0])
                  for tb in range(2)]
            release(t0)
            return PO(lambda e: e.tensor_tensor(sg[:, :, :], sg[:, :, :], sg[:, :, :], ALU.mult), t0)

        w_up, w_down = a["w_up"][0], a["w_down"][0]
        used_h = {"2": list(flat([opo.read])), "3": [use3["end"], t_pc, use2["end"]]}

        def up(s):
            nm = "23"[s % 2]
            op = operand(nm, [])
            for i in range(4):
                gemm(opm, w_up, 0, 2048 * s + 512 * i, 512, range(16), hidden(op, 4 * i, used_h[nm], relu2))
            return op

        def down(s, op):
            for n in range(4):
                gemm(op, w_down, 2048 * s, 512 * n, 512, range(16), residual(n, s == 3))
            used_h["23"[s % 2]] = op.read

        MD["acc"][2:4] = [use3["end"], use3["end"]]
        mods_more(0, 8)
        MD["rate"] = MR2
        ho = up(0)
        for s in range(1, 4):
            nx = up(s)
            down(s - 1, ho)
            ho = nx
        mods_finish()
        t_g2 = []
        g_x = gmod[:, 0, :]
        t_a = ts(g_x, modx[:, 16:32], 1.0, None, ALU.add, None, MD["xdone"])
        t_g2.append(tt(g_x, g_x, gain["mix2"], ALU.mult, t_a, t_cols))
        ctxx = sb_ctx
        t_ctx = load(ctxx[:, :, :], a["ctx_2"][0].rearrange("(t p) d -> p t d", p=128), opm.read, q=PO)
        rs = stats(ctxx, t_ctx, st[:, 6:8])
        opc = operand("2", [])
        turn(ctxx, lambda q, tb: t_ctx, rs, opc, g_x, modx[:, 0:16], [t_g2, MD["xdone"]], used_h["2"], rest=2, ease=True)
        lanes["small"].append(opc.gen)
        down(3, ho)
        drain("small")
        ctx_used = list(flat([XN["free"]]))

        t_fn = load(gt[:, :], a["final_norm"].rearrange("(a n) -> a n", a=1).broadcast_to([128, D]), use3["end"], t_mk, t_mv,
                    opo.tok, q=PO)
        rs8 = sums(st[:, 8:10], RES["ss"])
        RES["ss"] = []
        t_gt0 = []

        def final_norm():
            yield
            yield
            for n in range(4):
                for tb in range(2):
                    xs = x[:, tb, 512 * n:512 * n + 512]
                    t1 = DV(lambda e, tb=tb, n=n, xs=xs: e.scalar_tensor_tensor(
                        out=xs, in0=xs, scalar=st[:, 8 + tb:9 + tb], in1=gt[:, 512 * n:512 * n + 512],
                        op0=ALU.mult, op1=ALU.mult), rs8[tb][1], t_fn, RES["tok"][2 * n + tb])
                    t2 = act(yb[tb][:, :], xs, ACT.Square, t1, XN["yb"][tb], accum_out=ssp[:, tb, n:n + 1])
                    XN["yb"][tb] = [t2]
                    RES["ss"].append(t2)
                    RES["tok"][2 * n + tb] = [t1, t2]
                    t_gt0.append(t1)
                yield
            rs = sums(st[:, 10:12], RES["ss"])
            RES["ss"] = []
            yield
            turn(x, lambda q, tb: RES["tok"][2 * q + tb], rs, op1, g_l, mod[:, 0:16], [t_gl, MD["done"]],
                 [opm.read, ctx_used], ease=True)
            yield from op1.gen

        t_cst2 = [load(ropc[:, :, :], cd[:, ROC:ROC + 256].rearrange("p (a b) -> p a b", a=2), t_sv, t_ln, use["end"], op2m.tok, q=PO),
                  load(rops[:, :, :], cd[:, ROS:ROS + 256].rearrange("p (a b) -> p a b", a=2), q=PO),
                  load(chm[:, :], cd[:, HGM + 768:HGM + 772], q=PO),
                  load(hgm[:, :, :], cd[:, HGM:HGM + 768].rearrange("p (a b) -> p a b", a=6), q=PO)]

        def gate_rows(c0, used):
            MD["gt"] = []

            def run():
                for q in range(4):
                    while not eb.ready():
                        yield
                    k, e, fr = eb.take()
                    for i in range(4):
                        c = c0 + 4 * q + i
                        t = mm(e[:, 128 * i:128 * i + 128], mod[:, c:c + 1].broadcast_to([128, 128]), ident[:, :],
                               True, True, MD["done"], fr, inc=(i == 3))
                    t1 = act(gt[:, 512 * q:512 * q + 512], e[:, :], ACT.Copy, t, used)
                    MD["gt"].append(t1)
                    eb.give(k, [t1])
                    yield
            spawn("small", run())

        g_l = gmod[:, 1, :]
        t_a = ts(g_l, mod[:, 16:32], 1.0, None, ALU.add, None, MD["done"])
        t_gl = tt(g_l, g_l, gain["mix2"], ALU.mult, t_a, t_cols)
        op1 = operand("1", [])
        op1.pieces = 0
        spawn("small", final_norm())

        w2 = a["w_in_2"][0]
        G = {"free": [list(ctx_used), ho.read], "lbfree": ho.read, "hv": [], "hq": []}
        tS0 = []

        def bounds(g, d, used):
            c0 = 512 * g
            t1 = load(lb[:, 0, :], a["hg_lb_2"][0, d:d + 1, c0:c0 + 512].broadcast_to([128, 512]), used, q=PO)
            t2 = load(lb[:, 1, :], a["hg_lb_2"][1, d:d + 1, c0:c0 + 512].broadcast_to([128, 512]), used, q=PO)
            t3 = tt(lb[:, 0, :], lb[:, 0, :], lb[:, 1, :], ALU.subtract, t1, t2)
            t4 = act(lb[:, 1, :], lb[:, 0, :], ACT.Sigmoid, t3, scale=-1.0)
            return [t4, act(lb[:, 0, :], lb[:, 0, :], ACT.Sigmoid, t4)]

        def forget(p, t, release, g, d, latl):
            while op1.pieces < 8:
                yield
            tb_ = bounds(g, d, G["lbfree"])
            fr = [G["free"], XN["free"], XN["yb"]]
            t0 = [act(hA[:, tb, :], p[tb][:, :], ACT.Sigmoid, t, fr) for tb in range(2)]
            release(t0)
            t1 = tt(hA[:, :, :], hA[:, :, :], lb[:, 1, :].unsqueeze(1).broadcast_to([128, 2, 512]), ALU.mult, t0, tb_)
            t2 = tt(hA[:, :, :], hA[:, :, :], lb[:, 0, :].unsqueeze(1).broadcast_to([128, 2, 512]), ALU.add, t1)
            G["lbfree"] = [t2]
            t3 = ts(hK[:, :, :], hA[:, :, :], -1.0, 1.0, ALU.mult, ALU.add, t2, fr)
            t4 = act(hA[:, :, :], hA[:, :, :], ACT.Ln, t2, t3)
            yield
            yield
            yield
            e3 = []
            for tb in range(2):
                k, e, fb = bb.take()
                if latl:
                    t5 = mm(e[:, :], hgm[:, 2 + d, :], hA[:, tb, :], True, True, t4, fb, t_cst2, inc=True)
                else:
                    far = tb == (0 if d == 0 else 1)
                    t5 = mm(e[:, :], hgm[:, 4 + d, :], hA[:, tb, :], True, not far, t4, fb, t_cst2, inc=not far)
                    if far:
                        t5 = mm(e[:, :], ones[:, :], hA[:, 1 - tb, :], False, True, inc=True)
                t6 = act(hE[:, tb, :], e[:, :], ACT.Exp, t5, fr)
                bb.give(k, [t6])
                e3.append(t6)
            t7 = tt(hE[:, :, :], hE[:, :, :], hK[:, :, :], ALU.mult, e3, t3)
            yield
            yield
            return t3, t4, t7

        def ctx_gate(g, d, hV, hv):
            def epi(p, t, release):
                def run():
                    t3, t4, t7 = yield from forget(p, t, release, g, d, False)
                    k, e, fb = bb.take()
                    for h in range(4):
                        for tb in range(2):
                            t8 = mm(e[:, 128 * h:128 * h + 128], hE[:, tb, 128 * h:128 * h + 128],
                                    hV[:, tb, 128 * h:128 * h + 128], tb == 0, tb == 1, t7, fb, hv,
                                    inc=(h == 3 and tb == 1))
                    t9 = act(S0[:, 8 * d + 4 * g:8 * d + 4 * g + 4, :], e[:, :].rearrange("p (a b) -> p a b", a=4),
                             ACT.Copy, t8, ctx_used)
                    bb.give(k, [t9])
                    tS0.append(t9)
                    G["free"] = [t8, t9]
                    yield
                spawn("big", run())
            return epi

        g0_used = list(flat([G["free"]]))
        for g in range(2):
            hv, hV = [], hVs[g]
            gemm(opc, w2, 0, 3072 + 512 * g, 512, range(16), to_rows(hV, 0, 512, 0, ACT.Copy, [g0_used, t_gt0], hv))
            for d in range(2):
                gemm(opc, w2, 0, 1024 + 1024 * d + 512 * g, 512, range(16), ctx_gate(g, d, hV, hv))
        t_qkg = []

        def qk_epi(nh, gi, dst, h0, rot, used, done):
            def epi(p, t, release):
                def run():
                    w = 128 * nh
                    while not stgs.ready():
                        yield
                    k, sg, fr = stgs.take()
                    rr = RT["free"]
                    ss = sm[:, 0:2 * nh].rearrange("p (a b) -> p a b", a=2)
                    t0 = [act(sg[:, tb, 0:w], p[tb][:, 0:w], ACT.Copy, t, fr) for tb in range(2)]
                    t1 = [act(rt[:, tb, 0:w], p[tb][:, 0:w], ACT.Square, t, rr) for tb in range(2)]
                    release(t0 + t1)
                    yield
                    v4 = lambda z, tb: z[:, tb, 0:w].rearrange("p (h d) -> p h d", h=nh)
                    t2 = [DV(lambda e, tb=tb: e.tensor_reduce(ss[:, tb, :], v4(rt, tb), AX, ALU.add), t1, rr)
                          for tb in range(2)]
                    s2 = sm[:, 0:2 * nh]
                    t3 = rstd_of(s2, 128, s2, t2)
                    t4 = [tt(v4(sg, tb), v4(sg, tb), bc(ss[:, tb, :], 128), ALU.mult, t3, t0) for tb in range(2)]
                    t5 = [tt(v4(sg, tb), v4(sg, tb), qkg[:, gi, :].unsqueeze(1).broadcast_to([128, nh, 128]),
                             ALU.mult, t4, t_qkg) for tb in range(2)]
                    yield
                    tl = t5
                    if rot:
                        t6 = []
                        for tb in range(2):
                            t6.append(tt(v4(rt, tb), v4(sg, tb), ropc[:, tb, :].unsqueeze(1).broadcast_to([128, nh, 128]),
                                         ALU.mult, t5, t_cst2, t2))
                            sv_ = sg[:, tb, 0:w].rearrange("p (h z f) -> p h z f", z=4, f=32)
                            dv_ = rt2[:, tb, 0:w].rearrange("p (h z f) -> p h z f", z=4, f=32)
                            rs_ = rops[:, tb, :].rearrange("p (z f) -> p z f", z=4)
                            for zz in range(4):
                                t6.append(tt(dv_[:, :, zz, :], sv_[:, :, zz ^ 1, :],
                                             rs_[:, zz, :].unsqueeze(1).broadcast_to([128, nh, 32]), ALU.mult, t5, rr))
                        tl = [tt(sg[:, :, 0:w], rt[:, :, 0:w], rt2[:, :, 0:w], ALU.add, t6)]
                        yield
                    RT["free"] = [tl]
                    yield
                    yield
                    for i in range(0, nh, 2):
                        while not eb.ready():
                            yield
                        kb, e, fb = eb.take()
                        for h in range(2):
                            for tb in range(2):
                                t7 = transpose(e[:, 256 * h + 128 * tb:256 * h + 128 * tb + 128],
                                               sg[:, tb, 128 * (i + h):128 * (i + h) + 128], tl, fb,
                                               inc=(h == 1 and tb == 1))
                        t8 = act(dst[:, h0 + i:h0 + i + 2, :], e[:, :].rearrange("p (a b) -> p a b", a=2), ACT.Copy, t7, used)
                        eb.give(kb, [t8])
                        done.append(t8)
                        yield
                    stgs.give(k, [t7])
                spawn("small", run())
            return epi

        RT = {}

        def load_qkg(used):
            t_qkg.clear()
            t_qkg.extend([load(qkg[:, 0, :], a["q_norm_g_2"].broadcast_to([128, 128]), used, q=PO),
                          load(qkg[:, 1, :], a["k_norm_g_2"].broadcast_to([128, 128]), used, q=PO)])

        t_xk, t_xv = [], []

        def ctx_kv(p, t, release):
            drain("big")
            RT["free"] = list(flat([G["free"], G["lbfree"]]))
            load_qkg(RT["free"])
            two(qk_epi(2, 1, xkT, 0, False, ctx_used, t_xk),
                to_rows(xv, 0, 256, 256, ACT.Copy, ctx_used, t_xv))(p, t, release)
        gemm(opc, w2, 0, 6144, 512, range(16), ctx_kv)
        op2m = operand("2", [])
        mix_used = opc.read

        E1R, E2R, STR, HSR = Ring(hE1), Ring(hE2), Ring(hST), Ring(hS)
        HMR = Ring(hM)
        HMR.free = [[MD["xdone"]], [MD["xdone"]]]
        HQ = {"tok": [], "free": [], "o": [], "ofree": []}

        def lat_gate(g, d, hQ, hV, hq, hv):
            def epi(p, t, release):
                def run():
                    t3, t4, t7 = yield from forget(p, t, release, g, d, True)
                    yield from until((hq, 2))
                    U = [dict(h=h, hs=slice(128 * h, 128 * h + 128)) for h in range(4)]

                    def turned(u):
                        h, hs = u["h"], u["hs"]
                        k, e, fb = bb.take()
                        for tb in range(2):
                            mm(e[:, 128 * tb:128 * tb + 128], hA[:, tb, hs], hgm[:, d, :], True, True, t4, fb, t_cst2)
                        for tb in range(2):
                            t5 = transpose(e[:, 256 + 128 * tb:384 + 128 * tb], hK[:, tb, hs], t3, inc=(tb == 1))
                        u["k1"], E1, f1 = E1R.take()
                        u["k2"], E2, f2 = E2R.take()
                        t6 = act(E1[:, :], e[:, 0:256], ACT.Exp, t5, f1, G["e"])
                        t8 = act(E2[:, :], e[:, 0:256], ACT.Exp, t5, f2, G["e"], scale=-1.0)
                        dsl = E1[:, :].rearrange("p (c t) -> p c t", t=32)[:, :, 31 if d == 0 else 0]
                        dd = dec[:, h % 2, :]
                        t9 = copy(dd, dsl, t6, G["dec"][h % 2])
                        t10 = tt(E2[:, :], e[:, 256:512], E2[:, :], ALU.mult, t8)
                        bb.give(k, [t6, t8, t10])
                        t11 = tt(E1[:, :], E1[:, :], hQ[:, h, :], ALU.mult, t9, t6, hq)
                        u.update(E1=E1, E2=E2, dd=dd, t9=t9, t10=t10, t11=t11)

                    def states(u):
                        h, hs, E1, E2, dd = u["h"], u["hs"], u["E1"], u["E2"], u["dd"]
                        kk, eU, fU = bb.take()
                        kk2, eU2, fU2 = bb.take()
                        tus = {}
                        for tb, bank, w in ((0, eU, fU), (1, eU2, fU2)):
                            km, VM, tm = u["vm"][tb]
                            tus[tb] = mm(bank[:, :], hE[:, tb, hs], VM[:, :, :], True, True, t7, w, tm, inc=True)
                            HMR.give(km, [tus[tb]])
                        k, e, fb = bb.take()
                        for tb in range(2):
                            t12 = mm(e[:, 128 * tb:128 * tb + 128], E2[:, 128 * tb:128 * tb + 128],
                                     E1[:, 128 * tb:128 * tb + 128], True, True, u["t10"], u["t11"], fb, inc=(tb == 1))
                        E2R.give(u["k2"], [t12])
                        u["ks"], ST, fs = STR.take()
                        t13 = tt(ST[:, :, :], e[:, 0:256].rearrange("p (a b) -> p a b", a=2),
                                 hgm[:, d, :].unsqueeze(1).broadcast_to([128, 2, 128]), ALU.mult, t12, fs, G["e"])
                        bb.give(k, [t13])
                        u["kh"], HS, fh = HSR.take()
                        seq = list(range(8)) if d == 0 else list(range(7, -1, -1))
                        tc = copy(HS[:, seq[0], :], S0[:, 8 * d + 4 * g + h, :], fh, tS0, G["e"])
                        for c in seq[:7]:
                            tb = c // 4
                            bank, tu = (eU, eU2)[tb], tus[tb]
                            col = 128 * (c % 4)
                            nx = seq[seq.index(c) + 1]
                            tc = DV(lambda e_, c=c, nx=nx, bank=bank, col=col, dd=dd, HS=HS: e_.scalar_tensor_tensor(
                                out=HS[:, nx, :], in0=HS[:, c, :], scalar=dd[:, c:c + 1], in1=bank[:, col:col + 128],
                                op0=ALU.mult, op1=ALU.add), tu, tc, u["t9"])
                        G["dec"][h % 2] = tc
                        bb.give(kk, [tc])
                        bb.give(kk2, [tc])
                        u.update(ST=ST, HS=HS, t13=t13, tc=tc)

                    def outputs(u):
                        h, hs, E1, ST, HS = u["h"], u["hs"], u["E1"], u["ST"], u["HS"]
                        k, e, fb = bb.take()
                        for tb in range(2):
                            mm(e[:, 128 * tb:128 * tb + 128], hV[:, tb, hs], ST[:, tb, :], tb == 0, False, u["t13"], fb, hv)
                        for i, c in enumerate(range(8)):
                            t14 = mm(e[:, 32 * c:32 * c + 32], HS[:, c, :], E1[:, 32 * c:32 * c + 32], False, i == 7,
                                     u["tc"], inc=(i == 7))
                        STR.give(u["ks"], [t14])
                        HSR.give(u["kh"], [t14])
                        E1R.give(u["k1"], [t14])
                        if d == 0:
                            t15 = act(hO[:, h, :], e[:, 0:256], ACT.Copy, t14, HQ["ofree"])
                            HQ["o"][g].append(t15)
                        else:
                            t15 = tt(hO[:, h, :], e[:, 0:256], hO[:, h, :], ALU.add, t14, HQ["o"][g])
                            HQ["o2"][g].append(t15)
                        bb.give(k, [t15])
                        u["end"] = [t14, t15]

                    def masked(u):
                        u["vm"] = []
                        for tb in range(2):
                            km, VM, fm = HMR.take()
                            tm = PO(lambda e_, VM=VM, tb=tb, hs=u["hs"]: e_.tensor_tensor(
                                VM[:, :, :], hV[:, tb, hs].unsqueeze(1).broadcast_to([128, 4, 128]),
                                bc(chm[:, :], 128), ALU.mult), hv, fm, G["e"], t_cst2)
                            u["vm"].append((km, VM, tm))

                    for i in range(6):
                        if i >= 2:
                            outputs(U[i - 2])
                        if 1 <= i <= 4:
                            states(U[i - 1])
                        if i <= 3:
                            masked(U[i])
                            turned(U[i])
                        yield
                    t14, t15 = U[3]["end"]
                    G["free"] = [t14, t15]
                spawn("big", run())
            return epi

        def readout(g):
            def epi(p, t, release):
                def run():
                    while not stgs.ready():
                        yield
                    ks, sg, fr = stgs.take()
                    t0 = [act(sg[:, tb, :], p[tb][:, :], ACT.Silu, t, fr) for tb in range(2)]
                    release(t0)
                    yield
                    for i in range(2):
                        hh = slice(2 * i, 2 * i + 2)
                        A = hA[:, i, :]
                        A3 = A.rearrange("p (a b) -> p a b", a=2)
                        t1 = act(A3, hO[:, hh, :], ACT.Square, HQ["o2"][g], G["free"])
                        yield
                        k, e, fb = bb.take()
                        t2 = mm(e[:, :], ones[:, :], A, True, True, t1, fb, inc=True)
                        t3 = ts(A, e[:, :], 1.0 / 128, EPS, ALU.mult, ALU.add, t2)
                        bb.give(k, [t3])
                        t4 = act(A, A, ACT.Sqrt, t3)
                        t5 = recip(A, A, t4)
                        t6 = DV(lambda e, A3=A3, hh=hh: e.scalar_tensor_tensor(
                            out=A3, in0=hO[:, hh, :], scalar=hgn, in1=A3, op0=ALU.mult, op1=ALU.mult), t5, t_cols2)
                        yield
                        yield
                        kb, e, fb = bb.take()
                        for h in range(2):
                            for tb in range(2):
                                t7 = transpose(e[:, 256 * h + 128 * tb:256 * h + 128 * tb + 128],
                                               sg[:, tb, 128 * (2 * i + h):128 * (2 * i + h) + 128], t0, fb,
                                               inc=(h == 1 and tb == 1))
                        t8 = tt(A, A, e[:, :], ALU.mult, t6, t7)
                        bb.give(kb, [t8])
                        kt = 4 * g + 2 * i
                        tk = split(op2m, [kt, kt + 1], 0, S, A3, t8, mix_used)
                        G["free"] = [G["free"], tk]
                        HQ["ofree"] = [HQ["ofree"], t6]
                        yield
                    stgs.give(ks, [t7])
                spawn("big", run())
            return epi

        G["dec"] = [None, None]

        def settled(epi):
            def run(p, t, release):
                drain("small")
                G["free"] = [G["free"], RT["free"]]
                G["lbfree"] = [G["lbfree"], RT["free"]]
                G["e"] = [list(flat([G["free"]]))]
                g0_used.extend(flat([G["free"]]))
                HQ["ofree"] = [RT["free"]]
                epi(p, t, release)
            return run
        HQ["o"], HQ["o2"] = [[], []], [[], []]
        for g in range(2):
            hv, hq, hV, hQ = [], [], hVs[g], hQs[g]
            gu = [g0_used, t_gt0]
            rows_v = to_rows(hV, 0, 512, 0, ACT.Copy, gu, hv)
            gemm(op1, w2, 0, 3072 + 512 * g, 512, range(16), rows_v if g else settled(rows_v))
            gemm(op1, w2, 0, 512 * g, 512, range(16), to_heads(hQ, 0, ACT.Silu, used=gu, done=hq))
            for d in range(2):
                gemm(op1, w2, 0, 1024 + 1024 * d + 512 * g, 512, range(16), lat_gate(g, d, hQ, hV, hq, hv))
            gemm(op1, w2, 0, 4096 + 512 * g, 512, range(16), readout(g))

        t_lk, t_lv, t_lq, end = [], [], [], []

        def lat_kv(p, t, release):
            drain("big")
            end.extend(flat([G["free"], G["lbfree"], HQ["ofree"]]))
            RT["free"] = list(end)
            load_qkg(end)
            two(qk_epi(2, 1, lkT, 0, True, end, t_lk), to_rows(lv, 0, 256, 256, ACT.Copy, end, t_lv))(p, t, release)
        gemm(op1, w2, 0, 6144, 512, range(16), lat_kv)
        gemm(op1, w2, 0, 5120, 512, range(16), qk_epi(4, 0, lq, 0, True, end, t_lq))
        gemm(op1, w2, 0, 5632, 512, range(16), qk_epi(4, 0, lq, 4, True, end, t_lq))
        nsk = sm2[:, 0:8]
        t_nsk = ts(nsk, sink[:, :], -1.0, None, ALU.mult, None, t_sink)
        use4 = {"scr": [end], "op": mix_used}
        keys = lambda h, tb: [(lkT[:, h // 4, :], 0), (xkT[:, h // 4, :], 256)]
        vals = lambda h, b: (lv if b < 2 else xv)[:, b % 2, 128 * (h // 4):128 * (h // 4) + 128]
        spawn("big", after(attention(
            8, lambda h, tb: lq[:, h, 128 * tb:128 * tb + 128],
            [dict(k=keys, off=0, n=lambda tb: 512, mask=lambda tb: (mskt[:, 384:896] if tb == 0 else mskt[:, 0:512]),
                  slot=0, v=vals, nkb=lambda tb: 4, tok=[t_lk, t_xk, t_c], vtok=[t_lv, t_xv])],
            op2m, 8, use4, t_lq, snk=(sink, nsk, [t_nsk, t_sink])), (t_lk, 1), (t_lv, 2), (t_lq, 4)))
        gate_rows(32, [G["free"], t_gt0])
        wo2 = a["w_out_2"][0]
        for n in range(4):
            gemm(op2m, wo2, 0, 512 * n, 512, range(8), residual(n, False, scale=gt))
        drain("big")
        XN["free"] = [[use4["end"]] for _ in range(4)]
        XN["yb"] = [[use4["end"]], [use4["end"]]]
        for n in range(4):
            gemm(op2m, wo2, 1024, 512 * n, 512, range(8, 16), residual(n, True, scale=gt))

        t_gtu = [list(t) for t in RES["tok"]]
        t_a = ts(gmod[:, 0, :], mod[:, 64:80], 1.0, None, ALU.add, None, MD["done"], opc.tok)
        t_gf = tt(gmod[:, 0, :], gmod[:, 0, :], gain["ffn2"], ALU.mult, t_a, t_cols)
        opf = norm_turn("1", op1.read, gmod[:, 0, :], mod[:, 48:64], [t_gf, MD["done"]])
        mods_start(20, 24, "col", 0.33)
        MD["credit"] = -4.0
        wgu, wd2 = a["w_gate_up_2"][0], a["w_down_2"][0]
        used_h = {"2": list(flat([op2m.read])), "3": [use4["end"]] + op2m.read}

        def gate_up(s, cnt):
            nm = "23"[s % 2]
            op = operand(nm, [])
            for i in range(cnt):
                cell = {}

                def epi_g(p, t, release, cell=cell):
                    def run():
                        while not stgs.ready():
                            yield
                        cell["k"], sg, fr = stgs.take()
                        cell["sg"] = sg
                        cell["t"] = [act(sg[:, tb, :], p[tb][:, :], ACT.Silu, t, fr) for tb in range(2)]
                        release(cell["t"])
                    spawn("small", run())

                def epi_p(p, t, release, cell=cell, i=i):
                    def run():
                        sg = cell["sg"]
                        t1 = [tt(sg[:, tb, :], p[tb][:, :], sg[:, tb, :], ALU.mult, t, cell["t"]) for tb in range(2)]
                        release(t1)
                        yield
                        yield
                        for q in range(0, 4, 2):
                            while not eb.ready():
                                yield
                            kb, e, fb = eb.take()
                            for h in range(2):
                                for tb in range(2):
                                    t2 = transpose(e[:, 256 * h + 128 * tb:256 * h + 128 * tb + 128],
                                                   sg[:, tb, 128 * (q + h):128 * (q + h) + 128], t1, fb,
                                                   inc=(h == 1 and tb == 1))
                            eb.give(kb, split(op, [4 * i + q, 4 * i + q + 1], 0, S,
                                              e[:, :].rearrange("p (a b) -> p a b", a=2), t2, used_h[nm]))
                            yield
                        stgs.give(cell["k"], [t2])
                    spawn("small", run())
                gemm(opf, wgu, 0, 2048 * s + 512 * i, 512, range(16), epi_g)
                gemm(opf, wgu, 0, FF2 + 2048 * s + 512 * i, 512, range(16), epi_p)
            return op

        def down2(s, op, cnt, out=None):
            for n in range(4):
                gemm(op, wd2, 2048 * s, 512 * n, 512, range(4 * cnt), residual(n, False, scale=gt, out=out))
            used_h["23"[s % 2]] = op.read

        cnts = [4, 4, 3]
        ho = gate_up(0, 4)
        for s in range(1, 3):
            nx = gate_up(s, cnts[s])
            if s == 1:
                mods_finish()
                gate_rows(80, t_gtu)
            down2(s - 1, ho, cnts[s - 1])
            ho = nx
        down2(2, ho, 3, out=a["out"])
        return rec, dict(PE=PE, AC=AC, DV=DV, PO=PO, SP=SP)

    bmc = small("bmc", [96])
    sm2 = small("sm2", [8])

    mk_t, mv_t = mk, mv
    sb_ctx = sb("ctxx", rT1, [2, D])

    plan, _ = emit(None)
    _, q = emit(plan)

    with nc.Block() as block:
        @block.sync
        def _(eng):
            q["SP"].replay(eng)
            eng.wait_ge(s_out, 16 * 8)

        @block.scalar
        def _(eng):
            q["AC"].replay(eng)

        @block.vector
        def _(eng):
            q["DV"].replay(eng)

        @block.gpsimd
        def _(eng):
            q["PO"].replay(eng)

        @block.tensor
        def _(eng):
            q["PE"].replay(eng)


_INS = ['x', 'mem', 'norm_mix', 'w_in', 'gmlp_ln_g', 'gmlp_ln_b', 'gmlp_w_s', 'gmlp_b_s', 'cmp_pos', 'cmp_k_w1',
        'cmp_k_w2', 'cmp_v_w1', 'cmp_v_w2', 'w_out', 'norm_xattn', 'norm_mem', 'xattn_wq', 'xattn_wkv', 'xattn_wo',
        'norm_mlp', 'w_up', 'w_down', 'final_norm', 'c_2', 'ctx_2', 'c_ctx_2', 'w_mod_2', 'b_mod_2', 'norm_mix_g_2',
        'norm_ffn_g_2', 'w_in_2', 'hg_lb_2', 'hg_norm_g_2', 'q_norm_g_2', 'k_norm_g_2', 'attn_sink_2', 'w_out_2',
        'w_gate_up_2', 'w_down_2']


def kernel(**inputs):
    from concourse import bacc
    from concourse.bass_utils import run_bass_kernel_spmd

    nc = bacc.Bacc("TRN2", target_bir_lowering=False, num_devices=1)
    arrays, args = {}, {}
    for name in _INS:
        arr = np.ascontiguousarray(inputs[name])
        arrays["in_" + name] = arr
        args[name] = nc.dram_tensor("in_" + name, arr.shape, F, kind="ExternalInput").ap()
    arrays["in_consts"] = constants()
    args["consts"] = nc.dram_tensor("in_consts", (128, NCONST), F, kind="ExternalInput").ap()
    args["out"] = nc.dram_tensor("out_0", (1, S, D), F, kind="ExternalOutput").ap()
    program(nc, args)
    r = run_bass_kernel_spmd(nc, [arrays], core_ids=[0])
    return r.results[0]["out_0"]
```
